# Optimizing a Trainium2 kernel written in Bass

```python
import math
import jax, jax.numpy as jnp
from jax import lax
import numpy as np

D_MODEL = 1024
BATCH = 1
SEQ = 1024
DEPTH = 2

N_MIXERS = 2
N_ATTN_LAYERS = (DEPTH + 1) // 2
N_MLSTM_LAYERS = DEPTH // 2

ATTN_HEADS = 16
ATTN_HEAD_DIM = D_MODEL // ATTN_HEADS
DILATION_PATTERNS = ((128, 1), (512, 4), (2048, 16))
N_GROUPS = len(DILATION_PATTERNS)
ATTN_GROUP_WIDTH = ATTN_HEADS * ATTN_HEAD_DIM
ATTN_IN_WIDTH = 3 * N_GROUPS * ATTN_GROUP_WIDTH
REL_BUCKETS = 32
REL_MAX_DISTANCE = 2048

MLSTM_HEADS = 4
MLSTM_V_DIM = D_MODEL // MLSTM_HEADS
MLSTM_QK_DIM = MLSTM_V_DIM // 2
MLSTM_CHUNK = 64
CONV_WIDTH = 4
MLSTM_QK_WIDTH = 2 * MLSTM_HEADS * MLSTM_QK_DIM
MLSTM_VW = MLSTM_HEADS * MLSTM_V_DIM
MLSTM_IN_WIDTH = MLSTM_QK_WIDTH + MLSTM_VW + D_MODEL + 2 * MLSTM_HEADS

D_FF = 4 * D_MODEL
EPS = 1e-6

kernel_name = "hybrid_dilated_attn_mlstm_trunk"

def rms_norm(x, g):
    xf = x.astype(jnp.float32)
    y = xf * lax.rsqrt(jnp.mean(xf * xf, axis=-1, keepdims=True) + EPS)
    return (y * g.astype(jnp.float32)).astype(x.dtype)

def t5_bucket(dist):
    max_exact = REL_BUCKETS // 2
    d = jnp.maximum(dist.astype(jnp.float32), 1.0)
    large = max_exact + (jnp.log(d / max_exact) / math.log(REL_MAX_DISTANCE / max_exact)
                         * (REL_BUCKETS - max_exact)).astype(jnp.int32)
    large = jnp.minimum(large, REL_BUCKETS - 1)
    return jnp.where(dist < max_exact, dist, large)

def dilated_window_attention(q, k, v, rel_bias, window, dilation):
    b, s, h, e = q.shape
    band = window // dilation
    span = band * dilation
    s_pad = -(-s // span) * span
    n_blk = s_pad // span

    def to_blocks(t):
        t = jnp.pad(t, ((0, 0), (0, s_pad - s), (0, 0), (0, 0)))
        return t.reshape(b, n_blk, band, dilation, h, e)

    def with_prev(t):
        prev = jnp.pad(t[:, :-1], ((0, 0), (1, 0), (0, 0), (0, 0), (0, 0), (0, 0)))
        return jnp.concatenate([prev, t], axis=2)

    qb = to_blocks(q)
    kk = with_prev(to_blocks(k))
    vv = with_prev(to_blocks(v))

    scores = jnp.einsum('bnqrhe,bnkrhe->bnrhqk', qb, kk)
    qi = jnp.arange(band)[:, None]
    ki = jnp.arange(2 * band)[None, :]
    steps = qi - ki + band
    valid = (steps >= 0) & (steps <= band)
    blk_valid = valid[None] & ((jnp.arange(n_blk)[:, None, None] > 0) | (ki >= band)[None])
    bias = jnp.transpose(rel_bias[t5_bucket(jnp.clip(steps, 0, band) * dilation)], (2, 0, 1))
    scores = scores + bias.astype(jnp.float32)[None, None, None]
    scores = jnp.where(blk_valid[None, :, None, None], scores, -jnp.inf)

    m = jnp.max(scores, axis=-1, keepdims=True)
    ex = jnp.exp(scores - m)
    den = jnp.sum(ex, axis=-1, keepdims=True)
    out = jnp.einsum('bnrhqk,bnkrhe->bnqrhe', ex / den, vv)
    lse = (m + jnp.log(den))[..., 0]
    out = out.reshape(b, s_pad, h, e)[:, :s]
    lse = jnp.transpose(lse, (0, 1, 4, 2, 3)).reshape(b, s_pad, h)[:, :s]
    return out, lse

def attention_mixer(x, w_in, q_gain, k_gain, w_out, rel_bias):
    b, s, _ = x.shape
    qkv = (x @ w_in).astype(jnp.float32).reshape(b, s, 3, N_GROUPS, ATTN_HEADS, ATTN_HEAD_DIM)
    outs, lses = [], []
    for g, (window, dilation) in enumerate(DILATION_PATTERNS):
        q = rms_norm(qkv[:, :, 0, g], q_gain[g]) * (ATTN_HEAD_DIM ** -0.5)
        k = rms_norm(qkv[:, :, 1, g], k_gain[g])
        o, l = dilated_window_attention(q, k, qkv[:, :, 2, g], rel_bias[:, g], window, dilation)
        outs.append(o)
        lses.append(l)
    wts = jax.nn.softmax(jnp.stack(lses), axis=0)
    y = jnp.einsum('gbsh,gbshe->bshe', wts, jnp.stack(outs))
    return y.reshape(b, s, ATTN_GROUP_WIDTH).astype(x.dtype) @ w_out

def causal_depthwise_conv(x, w, bias):
    y = lax.conv_general_dilated(x, w[:, None, :].astype(x.dtype), window_strides=(1,),
                                 padding=[(CONV_WIDTH - 1, 0)],
                                 dimension_numbers=('NWC', 'WIO', 'NWC'),
                                 feature_group_count=x.shape[-1])
    return y + bias.astype(x.dtype)

def mlstm_chunkwise(q, k, v, log_i, log_f):
    b, h, s, dk = q.shape
    dv = v.shape[-1]
    L = MLSTM_CHUNK
    nc = s // L

    def chunks(t):
        return jnp.moveaxis(t.reshape(b, h, nc, L, *t.shape[3:]), 2, 0)

    causal = jnp.tril(jnp.ones((L, L), dtype=bool))

    def step(carry, xs):
        c_prev, n_prev, m_prev = carry
        qc, kc, vc, ic, fc = xs
        bcum = jnp.cumsum(fc, axis=-1)
        d = jnp.where(causal, bcum[..., :, None] - bcum[..., None, :] + ic[..., None, :], -jnp.inf)
        m_t = jnp.maximum(bcum + m_prev[..., None], jnp.max(d, axis=-1))
        inter = jnp.exp(bcum + m_prev[..., None] - m_t)
        wts = jnp.einsum('bhtd,bhsd->bhts', qc, kc) * jnp.exp(d - m_t[..., None])
        num = inter[..., None] * jnp.einsum('bhvd,bhtd->bhtv', c_prev, qc) + jnp.einsum('bhts,bhsv->bhtv', wts, vc)
        den = inter * jnp.einsum('bhd,bhtd->bht', n_prev, qc) + jnp.sum(wts, axis=-1)
        hc = num / jnp.maximum(jnp.abs(den), jnp.exp(-m_t))[..., None]
        b_last = bcum[..., -1]
        a = b_last[..., None] - bcum + ic
        m_new = jnp.maximum(b_last + m_prev, jnp.max(a, axis=-1))
        decay = jnp.exp(b_last + m_prev - m_new)
        wk = jnp.exp(a - m_new[..., None])
        c_new = decay[..., None, None] * c_prev + jnp.einsum('bhs,bhsv,bhsd->bhvd', wk, vc, kc)
        n_new = decay[..., None] * n_prev + jnp.einsum('bhs,bhsd->bhd', wk, kc)
        return (c_new, n_new, m_new), hc

    init = (jnp.zeros((b, h, dv, dk), jnp.float32), jnp.zeros((b, h, dk), jnp.float32),
            jnp.zeros((b, h), jnp.float32))
    _, hs = lax.scan(step, init, (chunks(q), chunks(k), chunks(v), chunks(log_i), chunks(log_f)))
    return jnp.moveaxis(hs, 0, 2).reshape(b, h, s, dv)

def mlstm_mixer(x, w_in, gate_bias, conv_w, conv_b, out_gain, w_out):
    b, s, _ = x.shape
    hh = MLSTM_HEADS
    proj = x @ w_in
    qk, v, o_pre, gates = jnp.split(proj, [MLSTM_QK_WIDTH, MLSTM_QK_WIDTH + MLSTM_VW,
                                           MLSTM_QK_WIDTH + MLSTM_VW + D_MODEL], axis=-1)
    qk = jax.nn.silu(causal_depthwise_conv(qk, conv_w, conv_b))
    q, k = jnp.split(qk, 2, axis=-1)
    gates = gates.astype(jnp.float32) + gate_bias.astype(jnp.float32)
    log_i = jnp.transpose(gates[..., :hh], (0, 2, 1))
    log_f = jnp.transpose(jax.nn.log_sigmoid(gates[..., hh:]), (0, 2, 1))

    def heads(t, dh):
        return jnp.transpose(t.astype(jnp.float32).reshape(b, s, hh, dh), (0, 2, 1, 3))

    hcell = mlstm_chunkwise(heads(q, MLSTM_QK_DIM) * (MLSTM_QK_DIM ** -0.5), heads(k, MLSTM_QK_DIM),
                            heads(v, MLSTM_V_DIM), log_i, log_f)
    hcell = rms_norm(jnp.transpose(hcell, (0, 2, 1, 3)), out_gain)
    y = hcell.reshape(b, s, MLSTM_VW) * jax.nn.sigmoid(o_pre.astype(jnp.float32))
    return y.astype(x.dtype) @ w_out

def sq_relu_mlp(x, w1, w2):
    hid = jax.nn.relu(x @ w1)
    return (hid * hid) @ w2

def setup_inputs(seed: int = 0) -> dict:
    key = jax.random.key(seed)
    ks = jax.random.split(key, 20)
    f32 = jnp.float32
    res_scale = (2.0 * DEPTH) ** -0.5
    nrm = lambda k, shape, sc: jax.random.normal(k, shape, f32) * sc
    f_bias = jnp.linspace(3.0, 6.0, MLSTM_HEADS, dtype=f32)
    gate_bias = jnp.concatenate([
        nrm(ks[9], (N_MLSTM_LAYERS, MLSTM_HEADS), 0.1),
        f_bias[None] + nrm(ks[10], (N_MLSTM_LAYERS, MLSTM_HEADS), 0.1)], axis=-1)
    return {
        "x": nrm(ks[0], (BATCH, SEQ, D_MODEL), 1.0),
        "mixer_norm": 1.0 + nrm(ks[1], (DEPTH, D_MODEL), 0.02),
        "mlp_norm": 1.0 + nrm(ks[2], (DEPTH, D_MODEL), 0.02),
        "rel_bias": nrm(ks[3], (REL_BUCKETS, N_GROUPS, ATTN_HEADS), 0.5),
        "attn_w_in": nrm(ks[4], (N_ATTN_LAYERS, D_MODEL, ATTN_IN_WIDTH), D_MODEL ** -0.5),
        "attn_q_gain": 1.0 + nrm(ks[5], (N_ATTN_LAYERS, N_GROUPS, ATTN_HEAD_DIM), 0.02),
        "attn_k_gain": 1.0 + nrm(ks[6], (N_ATTN_LAYERS, N_GROUPS, ATTN_HEAD_DIM), 0.02),
        "attn_w_out": nrm(ks[7], (N_ATTN_LAYERS, ATTN_GROUP_WIDTH, D_MODEL), ATTN_GROUP_WIDTH ** -0.5 * res_scale),
        "mlstm_w_in": nrm(ks[8], (N_MLSTM_LAYERS, D_MODEL, MLSTM_IN_WIDTH), D_MODEL ** -0.5),
        "mlstm_gate_bias": gate_bias,
        "mlstm_conv_w": nrm(ks[11], (N_MLSTM_LAYERS, CONV_WIDTH, MLSTM_QK_WIDTH), CONV_WIDTH ** -0.5),
        "mlstm_conv_b": nrm(ks[12], (N_MLSTM_LAYERS, MLSTM_QK_WIDTH), 0.02),
        "mlstm_out_gain": 1.0 + nrm(ks[13], (N_MLSTM_LAYERS, MLSTM_HEADS, MLSTM_V_DIM), 0.02),
        "mlstm_w_out": nrm(ks[14], (N_MLSTM_LAYERS, MLSTM_VW, D_MODEL), MLSTM_VW ** -0.5 * res_scale),
        "mlp_w_in": nrm(ks[15], (DEPTH, D_MODEL, D_FF), D_MODEL ** -0.5),
        "mlp_w_out": nrm(ks[16], (DEPTH, D_FF, D_MODEL), D_FF ** -0.5 * res_scale),
    }

def reference(x, mixer_norm, mlp_norm, rel_bias, attn_w_in, attn_q_gain, attn_k_gain, attn_w_out,
              mlstm_w_in, mlstm_gate_bias, mlstm_conv_w, mlstm_conv_b, mlstm_out_gain, mlstm_w_out,
              mlp_w_in, mlp_w_out):
    for layer in range(DEPTH):
        j = layer // N_MIXERS
        hnorm = rms_norm(x, mixer_norm[layer])
        if layer % N_MIXERS == 0:
            x = x + attention_mixer(hnorm, attn_w_in[j], attn_q_gain[j], attn_k_gain[j],
                                    attn_w_out[j], rel_bias)
        else:
            x = x + mlstm_mixer(hnorm, mlstm_w_in[j], mlstm_gate_bias[j], mlstm_conv_w[j],
                                mlstm_conv_b[j], mlstm_out_gain[j], mlstm_w_out[j])
        x = x + sq_relu_mlp(rms_norm(x, mlp_norm[layer]), mlp_w_in[layer], mlp_w_out[layer])
    return x


_drawn_inputs = setup_inputs


def setup_inputs(seed=0):
    import zlib

    import numpy as np

    out = dict(_drawn_inputs(seed))
    spreads = {}
    factors = {'mixer_norm': 7.587,
     'mlp_norm': 3.364,
     'attn_q_gain': 8.0,
     'attn_k_gain': 8.0,
     'mlstm_conv_b': 200.0,
     'mlstm_out_gain': 186.36}
    for name, (base, spread) in spreads.items():
        noise = np.random.default_rng([zlib.crc32(name.encode()), seed]).standard_normal(out[name].shape)
        drawn = base * np.exp(spread * noise) if base else spread * noise
        out[name] = __import__('jax').numpy.asarray(drawn.astype(out[name].dtype))
    for name, factor in factors.items():
        out[name] = (out[name] * factor).astype(out[name].dtype)
    return out
```

```python
import math
from contextlib import ExitStack, contextmanager

import numpy as np

import concourse.bass as bass
from concourse import mybir

F32 = mybir.dt.float32
F32R = mybir.dt.float32r
ALU = mybir.AluOpType
ACT = mybir.ActivationFunctionType
AX = mybir.AxisListType

P = 128
DM = 1024
SEQ = 1024
KT = DM // P
TT = SEQ // P
HALF = 512
EPS = 1e-6

GROUPS = ((128, 1), (512, 4), (2048, 16))
NG = len(GROUPS)
HEADS = 16
HD = DM // HEADS
PAIRS = HEADS // 2
SECTIONS = PAIRS * NG
REL_BUCKETS = 32
REL_MAX = 2048
BIAS_LEN = 384
MASKED = -1.0e30

MH = 4
DK = 128
DV = 256
CHUNKS = SEQ // P

DFF = 4 * DM
FCH = DFF // DM


def bias_onehot():
    out = np.zeros((NG, REL_BUCKETS + 1, BIAS_LEN), np.float32)
    exact = REL_BUCKETS // 2
    for g, (window, dilation) in enumerate(GROUPS):
        band = window // dilation
        for x in range(BIAS_LEN):
            step = x - (P - 1)
            if step < 0 or step > band:
                out[g, REL_BUCKETS, x] = 1.0
                continue
            dist = step * dilation
            large = exact + int(np.float32(np.log(np.float32(max(dist, 1)) / np.float32(exact)))
                                / np.float32(math.log(REL_MAX / exact)) * np.float32(REL_BUCKETS - exact))
            out[g, dist if dist < exact else min(large, REL_BUCKETS - 1), x] = 1.0
    return out


def split_matmul(pe, out, a_hi, a_lo, b_hi, b_lo, first, last):
    pe.matmul(out, a_hi, b_hi, start=first, stop=False)
    pe.matmul(out, a_hi, b_lo, start=False, stop=False)
    return pe.matmul(out, a_lo, b_hi, start=False, stop=last)


def perm_view(ap, g, width):
    if g == 0:
        return ap
    return ap.rearrange("p (i r) -> p r i", r=GROUPS[g][1])


def perm_dest(buf, g, t0, width):
    if g == 0:
        return buf[:, t0:t0 + width]
    d = GROUPS[g][1]
    if g == 1:
        n, i0 = t0 // HALF, (t0 % HALF) // d
        return buf.rearrange("p (r n i) -> p r n i", r=d, n=2)[:, :, n, i0:i0 + width // d]
    return buf.rearrange("p (r i) -> p r i", r=d)[:, :, t0 // d:(t0 + width) // d]


def natural_view(buf, g):
    if g == 0:
        return buf
    if g == 1:
        return buf.rearrange("p (r n i) -> p n i r", r=4, n=2)
    return buf.rearrange("p (r i) -> p i r", r=16)


def split_tokens(ap, g):
    if g == 0:
        return ap
    if g == 1:
        return ap.rearrange("p (n i r) -> p n i r", n=2, r=4)
    return ap.rearrange("p (i r) -> p i r", r=16)



@contextmanager
def phase_semaphores(nc, prefix):
    made = []

    def sem(name):
        made.append(nc.alloc_semaphore(name=prefix + name))
        return made[-1]

    yield sem
    nc.clear_and_free_semaphores(made)
    nc.all_engine_barrier()


def norm_phase(nc, name, xT, x_dram, gain_dram, ones, hT_hi, hT_lo):
    with ExitStack() as ctx:
        sb = lambda n, s, d=F32: ctx.enter_context(nc.sbuf_tensor(f"{name}_{n}", s, d))
        sem = ctx.enter_context(phase_semaphores(nc, f"{name}_"))
        gain = sb("gain", [P, KT])
        squares = sb("squares", [P, 2, SEQ])
        total = sb("total", [P, SEQ])
        rstd = sb("rstd", [P, SEQ])
        ring = sb("ring", [P, 3, HALF])
        ps = ctx.enter_context(nc.psum_tensor(f"{name}_ps", [P, 2, HALF], F32))
        gain_in = sem("gain_in")
        x_in = [sem(f"x_in{k}") for k in range(KT)] if x_dram is not None else None
        squared, added, summed, mean_done = sem("squared"), sem("added"), sem("summed"), sem("mean_done")
        root_done, rstd_done = sem("root_done"), sem("rstd_done")
        scaled, hi_done, lo_done = sem("scaled"), sem("hi_done"), sem("lo_done")
        block = ctx.enter_context(nc.Block())

        @block.sync
        def _(sp):
            if x_dram is not None:
                for k in range(KT):
                    sp.dma_start(xT[:, k], x_dram[k * P:(k + 1) * P, :]).then_inc(x_in[k], 16)
            sp.dma_start(gain[:], gain_dram).then_inc(gain_in, 16)

        @block.scalar
        def _(act):
            for k in range(KT):
                if x_dram is not None:
                    act.wait_ge(x_in[k], 16)
                if k >= 2:
                    act.wait_ge(added, k - 1)
                act.activation(squares[:, k % 2], xT[:, k], ACT.Square).then_inc(squared, 1)
            for s in range(2):
                act.wait_ge(mean_done, s + 1)
                act.activation(rstd[:, s * HALF:(s + 1) * HALF], total[:, s * HALF:(s + 1) * HALF],
                               ACT.Sqrt).then_inc(root_done, 1)
            for i in range(2 * KT):
                s, k = divmod(i, KT)
                act.wait_ge(scaled, i + 1)
                act.copy(hT_hi[:, k, s * HALF:(s + 1) * HALF], ring[:, i % 3]).then_inc(hi_done, 1)

        @block.vector
        def _(dve):
            dve.wait_ge(squared, 1)
            dve.tensor_copy(total[:], squares[:, 0]).then_inc(added, 1)
            for k in range(1, KT):
                dve.wait_ge(squared, k + 1)
                dve.wait_ge(added, k)
                dve.tensor_tensor(total[:], total[:], squares[:, k % 2], ALU.add).then_inc(added, 1)
            for s in range(2):
                cols = slice(s * HALF, (s + 1) * HALF)
                dve.wait_ge(summed, 2)
                dve.tensor_scalar(total[:, cols], ps[:, s], 1.0 / DM, EPS, ALU.mult, ALU.add).then_inc(mean_done, 1)
            for s in range(2):
                cols = slice(s * HALF, (s + 1) * HALF)
                dve.wait_ge(root_done, s + 1)
                dve.reciprocal(rstd[:, cols], rstd[:, cols]).then_inc(rstd_done, 1)
            dve.wait_ge(gain_in, 16)
            for i in range(2 * KT):
                s, k = divmod(i, KT)
                cols = slice(s * HALF, (s + 1) * HALF)
                dve.wait_ge(rstd_done, s + 1)
                if i >= 3:
                    dve.wait_ge(lo_done, i - 2)
                dve.scalar_tensor_tensor(ring[:, i % 3], xT[:, k, cols], gain[:, k:k + 1], rstd[:, cols],
                                         ALU.mult, ALU.mult).then_inc(scaled, 1)

        @block.gpsimd
        def _(pool):
            for i in range(2 * KT):
                s, k = divmod(i, KT)
                cols = slice(s * HALF, (s + 1) * HALF)
                pool.wait_ge(hi_done, i + 1)
                pool.tensor_tensor(hT_lo[:, k, cols], ring[:, i % 3], hT_hi[:, k, cols].bitcast(F32),
                                   ALU.subtract).then_inc(lo_done, 1)
            pool.wait_ge(lo_done, 2 * KT)

        @block.tensor
        def _(pe):
            pe.wait_ge(added, KT)
            for s in range(2):
                mm = pe.matmul(ps[:, s], ones[:], total[:, s * HALF:(s + 1) * HALF], start=True, stop=True)
                mm.then_inc(summed, 1)



def constants_phase(nc, ones, ident, rel_bias, onehot, bias_dram):
    with ExitStack() as ctx:
        sb = lambda n, s, d=F32: ctx.enter_context(nc.sbuf_tensor(n, s, d))
        sem = ctx.enter_context(phase_semaphores(nc, ""))
        rel = sb("rel", [REL_BUCKETS + 1, NG * HEADS])
        hot = sb("hot", [REL_BUCKETS + 1, NG, BIAS_LEN])
        vec = sb("vec", [HEADS, NG, BIAS_LEN])
        ps = ctx.enter_context(nc.psum_tensor("bias_ps", [HEADS, NG, HALF], F32))
        rel_in, hot_in, filled, zeroed = sem("rel_in"), sem("hot_in"), sem("filled"), sem("zeroed")
        bias_mm, bias_copied, bias_out = sem("bias_mm"), sem("bias_copied"), sem("bias_out")
        block = ctx.enter_context(nc.Block())

        @block.sync
        def _(sp):
            sp.dma_start(rel[0:REL_BUCKETS, :], rel_bias.rearrange("b g h -> b (g h)")).then_inc(rel_in, 16)
            sp.dma_start(hot[:], onehot.rearrange("g b x -> b g x")).then_inc(hot_in, 16)
            sp.wait_ge(bias_copied, 1)
            sp.dma_start(bias_dram.rearrange("g h x -> h g x"), vec[:]).then_inc(bias_out, 16)
            sp.wait_ge(bias_out, 16)

        @block.gpsimd
        def _(pool):
            pool.memset(ones[:], 1.0)
            pool.memset(ident[:], 0.0).then_inc(zeroed, 1)
            pool.wait_ge(zeroed, 1)
            pool.affine_select(out=ident[:], in_=ident[:], compare_op=ALU.not_equal, fill=1.0,
                               base=0, pattern=[[-1, P]], channel_multiplier=1)

        @block.vector
        def _(dve):
            dve.memset(rel[REL_BUCKETS:REL_BUCKETS + 1, :], MASKED).then_inc(filled, 1)
            dve.wait_ge(bias_mm, NG)
            dve.tensor_copy(vec[:], ps[:, :, 0:BIAS_LEN]).then_inc(bias_copied, 1)

        @block.tensor
        def _(pe):
            pe.wait_ge(rel_in, 16)
            pe.wait_ge(hot_in, 16)
            pe.wait_ge(filled, 1)
            for g in range(NG):
                pe.matmul(ps[:, g, 0:BIAS_LEN], rel[:, g * HEADS:(g + 1) * HEADS], hot[:, g, :],
                          start=True, stop=True).then_inc(bias_mm, 1)



LOOP_FIRST = 4
LOOP_ROUND = 6
LOOP_COUNT = 3
LAST_SUPER = SECTIONS + 2


def run_supersteps(eng, step):
    for st in range(LOOP_FIRST):
        for j in range(TT):
            step(0, st, j)
    with eng.Fori(0, LOOP_COUNT) as i:
        for st in range(LOOP_FIRST, LOOP_FIRST + LOOP_ROUND):
            for j in range(TT):
                step(i, st, j)
    for st in range(LOOP_FIRST + LOOP_ROUND * LOOP_COUNT, LAST_SUPER + 1):
        for j in range(TT):
            step(0, st, j)


def attention_phase(nc, ident, hT_hi, hT_lo, wqkv, q_gain, k_gain, bias_dram, yT_dram):
    with ExitStack() as ctx:
        sb = lambda n, s, d=F32: ctx.enter_context(nc.sbuf_tensor(n, s, d))
        ps = lambda n, s: ctx.enter_context(nc.psum_tensor(n, s, F32))
        sem = ctx.enter_context(phase_semaphores(nc, ""))
        W3 = 3 * P
        raw = sb("raw", [P, 4, W3])
        w_hi = sb("w_hi", [P, 2, KT, W3], F32R)
        w_lo = sb("w_lo", [P, 2, KT, W3], F32R)
        gains = sb("gains", [P, 2, NG])
        qk_hi = sb("qk_hi", [P, 2, 2, SEQ], F32R)
        qk_lo = sb("qk_lo", [P, 2, 2, SEQ], F32R)
        vT = sb("vT", [P, 2, SEQ])
        v_hi = sb("v_hi", [P, 3, P], F32R)
        v_lo = sb("v_lo", [P, 3, P], F32R)
        sq = sb("sq", [P, 2 * P])
        qkn = sb("qkn", [P, 2, 2 * P])
        ss = sb("ss", [P, 4])
        var = sb("var", [P, 4])
        rs = sb("rs", [P, 4])
        held = sb("held", [P, 1])
        minus_half = sb("minus_half", [P, 4])
        bias = [sb(f"bias{g}", [P, 2, 2 * P if g < 2 else P]) for g in range(NG)]
        prob = sb("prob", [P, 2, 2, 2 * P])
        pT_hi = sb("pT_hi", [P, 2, 2 * P], F32R)
        pT_lo = sb("pT_lo", [P, 2, 2 * P], F32R)
        stat = sb("stat", [P, 2, 4 * TT])
        neg_max = sb("neg_max", [P, 2, 2 * TT])
        stat_rows = sb("stat_rows", [4 * TT, P])
        o_raw = [sb("o_g0", [P, 2, SEQ]), sb("o_g1", [P, 1, SEQ]), sb("o_g2", [P, 1, SEQ])]
        w_bc = sb("w_bc", [P, 2, SEQ])
        compact = sb("compact", [64, NG, 2, 2, 16])
        top = sb("top", [64, 2, 16])
        diff = sb("diff", [64, NG, 2, 16])
        grown = sb("grown", [64, NG, 2, 16])
        part = sb("part", [64, NG, 2, 16])
        den = sb("den", [64, 2, 16])
        share = sb("share", [64, NG, 2, 16])

        ps_qk = [ps(f"ps_qk{i}", [P, HALF]) for i in range(2)]
        ps_v = ps("ps_v", [P, HALF])
        ps_t = ps("ps_t", [P, HALF])
        ps_s = [ps(f"ps_s{h}", [P, HALF]) for h in range(2)]
        ps_p = ps("ps_p", [P, HALF])
        ps_o = ps("ps_o", [P, HALF])

        stat_dram = nc.dram_tensor("stat_dram", [NG, 2, 2, SEQ], F32, kind="Internal").ap()
        share_dram = nc.dram_tensor("share_dram", [NG, 2, SEQ], F32, kind="Internal").ap()

        raw_in = [sem(f"raw_in{i}") for i in range(4)]
        gains_in = sem("gains_in")
        bias_in = [sem(f"bias_in{g}") for g in range(NG)]
        w_hi_done, w_lo_done = sem("w_hi_done"), sem("w_lo_done")
        qk_mm, v_mm, turned = sem("qk_mm"), sem("v_mm"), sem("turned")
        scored, p_turned, pv_done = sem("scored"), sem("p_turned"), sem("pv_done")
        squared, reduced, rs_done, qkn_done = sem("squared"), sem("reduced"), sem("rs_done"), sem("qkn_done")
        var_done = sem("var_done")
        turn_hi, turn_lo = sem("turn_hi"), sem("turn_lo")
        vT_done = sem("vT_done")
        maxed, neg_done, exp_done = sem("maxed"), sem("neg_done"), sem("exp_done")
        p_hi_done, p_lo_done, o_done = sem("p_hi_done"), sem("p_lo_done"), sem("o_done")
        rows_done, rows_out = sem("rows_done"), sem("rows_out")
        compact_in = [sem(f"compact_in{g}") for g in range(2)]
        merge, diff_done, grown_done, share_done = sem("merge"), sem("diff_done"), sem("grown_done"), sem("share_done")
        share_out, wbc_in = sem("share_out"), [sem(f"wbc_in{i}") for i in range(2)]
        y_step, y_out = sem("y_step"), sem("y_out")
        set_done, half_set = sem("set_done"), sem("half_set")
        block = ctx.enter_context(nc.Block())

        def has_unit(st, j, back):
            return TT <= TT * st + j - back < TT * (SECTIONS + 1)

        def unit(st, j, back):
            sec, u = divmod(TT * (st - 1) + j - back, TT)
            return sec, u

        def has_prev(g, u):
            return u > 0 if g == 0 else (u % 2 == 1 if g == 1 else False)

        @block.sync
        def _(sp):
            sp.dma_start(gains[0:HD, 0, :], q_gain).then_inc(gains_in, 16)
            sp.dma_start(gains[HD:P, 0, :], q_gain).then_inc(gains_in, 16)
            sp.dma_start(gains[0:HD, 1, :], k_gain).then_inc(gains_in, 16)
            sp.dma_start(gains[HD:P, 1, :], k_gain).then_inc(gains_in, 16)
            for n in range(TT + 4):
                if n >= 4:
                    sp.wait_ge(w_lo_done, n - 3)
                sp.dma_start(raw[:, n % 4], wqkv[n]).then_inc(raw_in[n % 4], 16)

            def step(i, st, j):
                N = st + 6 * i
                T = TT * N + j
                if TT * st + j + 12 < TT * SECTIONS:
                    sp.wait_ge(w_lo_done, T + 9)
                    sp.dma_start(raw[:, j % 4], wqkv[T + 12]).then_inc(raw_in[j % 4], 16)
                if j == 2 and st < SECTIONS:
                    g, pair = st % NG, st // NG + 2 * i
                    if st >= NG:
                        sp.wait_ge(neg_done, TT * N - 2 * TT)
                    base = (g * HEADS + 2 * pair) * BIAS_LEN
                    if g < 2:
                        sp.dma_start(bias[g][:], bass.AP(bias_dram.tensor, base, [[1, P], [BIAS_LEN, 2], [1, 2 * P]]))\
                            .then_inc(bias_in[g], 16)
                    else:
                        sp.dma_start(bias[g][0:64], bass.AP(bias_dram.tensor, base, [[1, 64], [BIAS_LEN, 2], [1, P]]))\
                            .then_inc(bias_in[g], 16)
                        sp.dma_start(bias[g][64:P, :, 0:64],
                                     bass.AP(bias_dram.tensor, base + 64, [[1, 64], [BIAS_LEN, 2], [1, 64]]))\
                            .then_inc(bias_in[g], 16)
                if j == 2 and 2 <= st <= SECTIONS + 1 and (st - 2) % NG < 2:
                    g, pair = (st - 2) % NG, (st - 2) // NG + 2 * i
                    rows = 2 * pair + g + 1
                    sp.wait_ge(rows_done, rows)
                    sp.dma_start(stat_dram[g].rearrange("s h (u q) -> (s h u) q", q=P), stat_rows[:]).then_inc(rows_out, 16)
                    sp.wait_ge(rows_out, 16 * rows)
                    for s in range(2):
                        for h in range(2):
                            src = stat_dram[g, s, h]
                            if g == 0:
                                sp.dma_start(compact[:, g, s, h, :], src.rearrange("(p c) -> p c", c=16))\
                                    .then_inc(compact_in[g], 16)
                            else:
                                sp.dma_start(compact[:, g, s, h, :].rearrange("p (r c) -> p r c", r=4),
                                             src.rearrange("(r p c) -> p r c", r=4, c=4)).then_inc(compact_in[g], 16)
                if j == 5 and st >= 4 and (st - 4) % NG == 0:
                    pair = (st - 4) // NG + 2 * i
                    sp.wait_ge(share_done, pair + 1)
                    sp.dma_start(share_dram.rearrange("g h (p c) -> p (g h) c", c=16),
                                 share[:].rearrange("p g h c -> p (g h) c")).then_inc(share_out, 16)
                    sp.wait_ge(share_out, 16 * pair + 16)
                    for g in range(2):
                        for h in range(2):
                            sp.dma_start(w_bc[64 * h:64 * h + 64, g, :],
                                         share_dram[g, h:h + 1, :].to_broadcast([64, SEQ])).then_inc(wbc_in[g], 16)
                if j == 0 and st >= 5 and (st - 5) % NG == 0:
                    pair = (st - 5) // NG + 2 * i
                    sp.wait_ge(y_step, 5 * pair + 1)
                    for h in range(2):
                        sp.dma_start(w_bc[64 * h:64 * h + 64, 0, :],
                                     share_dram[2, h:h + 1, :].to_broadcast([64, SEQ])).then_inc(wbc_in[0], 16)
                if j == 5 and st >= 5 and (st - 5) % NG == 0:
                    pair, par = (st - 5) // NG + 2 * i, ((st - 5) // NG) % 2
                    sp.wait_ge(y_step, 5 * pair + 5)
                    sp.dma_start(yT_dram[pair], o_raw[0][:, par, :]).then_inc(y_out, 16)

            run_supersteps(sp, step)
            sp.wait_ge(y_out, 16 * PAIRS)

        @block.tensor
        def _(pe):
            def step(i, st, j):
                N = st + 6 * i
                T = TT * N + j
                U = T - TT
                par = st % 2
                if st < SECTIONS:
                    if st >= 1 or j >= 2:
                        pe.wait_ge(qkn_done, T - 1)
                    for k in range(KT):
                        if j == 0:
                            pe.wait_ge(w_hi_done, TT * N + k + 1)
                            pe.wait_ge(w_lo_done, TT * N + k + 1)
                        mm = split_matmul(pe, ps_qk[j % 2][:, 0:2 * P],
                                          hT_hi[:, k, j * P:(j + 1) * P], hT_lo[:, k, j * P:(j + 1) * P],
                                          w_hi[:, par, k, 0:2 * P], w_lo[:, par, k, 0:2 * P], k == 0, k == KT - 1)
                    mm.then_inc(qk_mm, 1)
                if (st >= 1 or j >= 1) and st <= SECTIONS:
                    if TT * st + j >= 2:
                        pe.wait_ge(turn_hi, T - 1)
                        pe.wait_ge(turn_lo, T - 1)
                    if TT * st + j - 1 < TT * SECTIONS:
                        pe.wait_ge(qkn_done, T)
                        for a in range(2):
                            mm = pe.transpose(ps_t[:, a * P:(a + 1) * P], qkn[:, (j - 1) % 2, a * P:(a + 1) * P], ident[:])
                    if st >= 1:
                        if j == 0:
                            pe.wait_ge(vT_done, 2 * N)
                        mm = pe.transpose(ps_t[:, 2 * P:3 * P], vT[:, (st - 1) % 2, j * P:(j + 1) * P], ident[:])
                    if j == 1 and st >= 2 and (st - 2) % NG < 2:
                        pe.wait_ge(exp_done, U - 1)
                        pe.wait_ge(neg_done, U - 1)
                        mm = pe.transpose(ps_t[0:4 * TT, 3 * P:4 * P], stat[:, (st - 2) % 2, :], ident[:])
                    mm.then_inc(turned, 1)
                if has_unit(st, j, 1):
                    sec, u = unit(st, j, 1)
                    g = sec % NG
                    pe.wait_ge(exp_done, U)
                    if has_unit(st, j, 2):
                        pe.wait_ge(p_hi_done, U - 1)
                        pe.wait_ge(p_lo_done, U - 1)
                    for h in range(2):
                        for b in range(0 if has_prev(g, u) else 1, 2):
                            c = (2 * b + h) * P
                            mm = pe.transpose(ps_p[:, c:c + P], prob[:, u % 2, h, b * P:(b + 1) * P], ident[:])
                    mm.then_inc(p_turned, 1)
                if st < SECTIONS:
                    half = j // 4
                    if j == 0 and st >= 1:
                        pe.wait_ge(vT_done, 2 * N)
                    if j == 4:
                        pe.wait_ge(vT_done, 2 * N + 1)
                    for k in range(2 * (j % 4), 2 * (j % 4) + 2):
                        mm = split_matmul(pe, ps_v[:], w_hi[:, par, k, 2 * P:3 * P], w_lo[:, par, k, 2 * P:3 * P],
                                          hT_hi[:, k, half * HALF:(half + 1) * HALF],
                                          hT_lo[:, k, half * HALF:(half + 1) * HALF], k == 0, k == KT - 1)
                    if j % 4 == 3:
                        mm.then_inc(v_mm, 1)
                if has_unit(st, j, 0):
                    sec, u = unit(st, j, 0)
                    g, sp_ = sec % NG, sec % 2
                    if j == 0:
                        pe.wait_ge(turn_hi, T)
                        pe.wait_ge(turn_lo, T)
                    if has_unit(st, j, 1):
                        pe.wait_ge(exp_done, U)
                    k0 = (u - 1) * P if has_prev(g, u) else u * P
                    c0 = 0 if has_prev(g, u) else P
                    for h in range(2):
                        rows = slice(HD * h, HD * h + HD)
                        mm = split_matmul(pe, ps_s[h][:, c0:2 * P],
                                          qk_hi[rows, sp_, 0, u * P:(u + 1) * P], qk_lo[rows, sp_, 0, u * P:(u + 1) * P],
                                          qk_hi[rows, sp_, 1, k0:(u + 1) * P], qk_lo[rows, sp_, 1, k0:(u + 1) * P],
                                          True, True)
                    mm.then_inc(scored, 1)
                if has_unit(st, j, 1):
                    sec, u = unit(st, j, 1)
                    g = sec % NG
                    whole = TT * sec + u
                    pe.wait_ge(p_hi_done, U)
                    pe.wait_ge(p_lo_done, U)
                    if has_unit(st, j, 2):
                        pe.wait_ge(o_done, U - 1)
                    first = 0 if has_prev(g, u) else 1
                    for b in range(first, 2):
                        slot = (whole - 1 + b) % 3
                        mm = split_matmul(pe, ps_o[:, 0:2 * P], v_hi[:, slot, :], v_lo[:, slot, :],
                                          pT_hi[:, b, :], pT_lo[:, b, :], b == first, b == 1)
                    mm.then_inc(pv_done, 1)

            run_supersteps(pe, step)

        @block.scalar
        def _(act):
            def hi_part(n, slot, par, k):
                act.copy(w_hi[:, par, k, :], raw[:, slot, :]).then_inc(w_hi_done, 1)

            act.wait_ge(set_done, 2)
            for k in range(KT):
                act.wait_ge(raw_in[k % 4], 16 * (k // 4 + 1))
                hi_part(k, k % 4, 0, k)

            def step(i, st, j):
                N = st + 6 * i
                T = TT * N + j
                U = T - TT
                par = st % 2
                if j == 0 and 1 <= st <= SECTIONS:
                    act.wait_ge(v_mm, 2 * N)
                    g, vp = (st - 1) % NG, (st - 1) % 2
                    act.copy(perm_dest(vT[:, vp, :], g, HALF, HALF), perm_view(ps_v[:], g, HALF)).then_inc(vT_done, 1)
                if j == 4 and st < SECTIONS:
                    act.wait_ge(v_mm, 2 * N + 1)
                    g = st % NG
                    act.copy(perm_dest(vT[:, par, :], g, 0, HALF), perm_view(ps_v[:], g, HALF)).then_inc(vT_done, 1)
                if has_unit(st, j, 1):
                    sec, u = unit(st, j, 1)
                    g, sp_ = sec % NG, sec % 2
                    act.wait_ge(neg_done, U)
                    if has_unit(st, j, 3):
                        act.wait_ge(p_turned, U - 2)
                    c0 = 0 if has_prev(g, u) else P
                    for h in range(2):
                        a = act.activation(prob[:, u % 2, h, c0:2 * P], ps_s[h][:, c0:2 * P], ACT.Exp,
                                           bias=neg_max[:, sp_, h * TT + u:h * TT + u + 1],
                                           accum_out=stat[:, sp_, (2 + h) * TT + u:(2 + h) * TT + u + 1])
                    a.then_inc(exp_done, 1)
                if has_unit(st, j, 2):
                    sec, u = unit(st, j, 2)
                    g = sec % NG
                    act.wait_ge(pv_done, U - 1)
                    if u == 0:
                        pair_st = sec // NG
                        if g == 0 and pair_st >= 2:
                            act.wait_ge(y_out, 16 * (pair_st + 2 * i) - 16)
                        if g >= 1 and pair_st >= 1:
                            act.wait_ge(y_step, 5 * (pair_st + 2 * i) - 5 + 2 * g)
                    ob = o_raw[g][:, (sec // NG) % 2 if g == 0 else 0, :]
                    act.copy(ob[0:HD, u * P:(u + 1) * P], ps_o[0:HD, 0:P])
                    act.copy(ob[HD:P, u * P:(u + 1) * P], ps_o[HD:P, P:2 * P]).then_inc(o_done, 1)
                if j == 3 and st >= 4 and (st - 4) % NG == 0:
                    act.wait_ge(diff_done, (st - 4) // NG + 2 * i + 1)
                    act.activation(grown[:], diff[:], ACT.Exp).then_inc(grown_done, 1)
                if st + 1 < SECTIONS:
                    if j == 0 and st >= 1:
                        act.wait_ge(qk_mm, TT * N)
                        act.wait_ge(v_mm, 2 * N)
                    act.wait_ge(raw_in[j % 4], 32 * N + 16 * (3 + j // 4))
                    hi_part(T, j % 4, (st + 1) % 2, j)
                if st < SECTIONS:
                    act.wait_ge(qk_mm, T + 1)
                    if TT * st + j >= 1:
                        act.wait_ge(reduced, T)
                    act.activation(sq[:], ps_qk[j % 2][:, 0:2 * P], ACT.Square).then_inc(squared, 1)
                if (st >= 1 or j >= 1) and st <= SECTIONS:
                    act.wait_ge(turned, T)
                    if TT * st + j - 1 < TT * SECTIONS:
                        sec, t = divmod(TT * st + j - 1, TT)
                        g = sec % NG
                        for a in range(2):
                            ins = act.activation(perm_dest(qk_hi[:, sec % 2, a, :], g, t * P, P),
                                                 perm_view(ps_t[:, a * P:(a + 1) * P], g, P), ACT.Copy,
                                                 scale=gains[:, a, g:g + 1])
                    if st >= 1:
                        ins = act.copy(v_hi[:, (TT * (st - 1) + j) % 3, :], ps_t[:, 2 * P:3 * P])
                    ins.then_inc(turn_hi, 1)
                if has_unit(st, j, 1):
                    sec, u = unit(st, j, 1)
                    b0 = 0 if has_prev(sec % NG, u) else 1
                    act.wait_ge(p_turned, U)
                    act.copy(pT_hi[:, b0:2, :],
                             ps_p[:].rearrange("p (b c) -> p b c", b=2)[:, b0:2, :]).then_inc(p_hi_done, 1)

            run_supersteps(act, step)

        @block.vector
        def _(dve):
            dve.memset(bias[2][64:P, :, 64:P], MASKED).then_inc(set_done, 1)
            dve.wait_ge(gains_in, 64)
            dve.tensor_scalar(gains[:, 0, :], gains[:, 0, :], HD ** -0.5, None, ALU.mult).then_inc(set_done, 1)
            def step(i, st, j):
                N = st + 6 * i
                T = TT * N + j
                U = T - TT
                if has_unit(st, j, 1):
                    sec, u = unit(st, j, 1)
                    g, sp_ = sec % NG, sec % 2
                    n = 2 * P if has_prev(g, u) else P
                    if u == 0:
                        per = 16 if g < 2 else 32
                        dve.wait_ge(bias_in[g], per * (sec // NG + 2 * i) + per)
                    dve.wait_ge(scored, U)
                    dve.memset(held[:], 0.0)
                    for h in range(2):
                        width = 2 * P if g < 2 else P
                        rev = bass.AP(bias[g][:].tensor, h * width + n - 1, [[2 * width, P], [-1, n]])
                        s = ps_s[h][:, 2 * P - n:2 * P]
                        dve.tensor_tensor_reduce(s, s, rev, 1.0, -3.0e38, ALU.add, ALU.max,
                                                 stat[:, sp_, h * TT + u:h * TT + u + 1]).then_inc(maxed, 1)
                    dve.wait_ge(maxed, 2 * U)
                    dve.tensor_scalar(neg_max[:, sp_, u:2 * TT:TT], stat[:, sp_, u:2 * TT:TT], -1.0, None,
                                      ALU.mult).then_inc(neg_done, 1)
                if st < SECTIONS:
                    dve.wait_ge(squared, T + 1)
                    if TT * st + j >= 1:
                        dve.wait_ge(var_done, T)
                    dve.tensor_reduce(ss[:], sq[:].rearrange("p (h e) -> p h e", e=HD), AX.X, ALU.add)\
                        .then_inc(reduced, 1)
                    dve.wait_ge(reduced, T + 1)
                    if TT * st + j >= 1:
                        dve.wait_ge(rs_done, T)
                    dve.tensor_scalar(var[:], ss[:], 1.0 / HD, EPS, ALU.mult, ALU.add).then_inc(var_done, 1)
                if (st >= 1 or j >= 1) and st <= SECTIONS:
                    dve.wait_ge(turn_hi, T)
                    if j == 1 and st >= 2 and (st - 2) % NG < 2:
                        if st >= 3:
                            dve.wait_ge(rows_out, 16 * (2 * ((st - 2) // NG + 2 * i) + (st - 2) % NG))
                        dve.tensor_copy(stat_rows[:], ps_t[0:4 * TT, 3 * P:4 * P]).then_inc(rows_done, 1)
                    if TT * st + j - 1 < TT * SECTIONS:
                        sec, t = divmod(TT * st + j - 1, TT)
                        g = sec % NG
                        for a in range(2):
                            ins = dve.scalar_tensor_tensor(
                                perm_dest(qk_lo[:, sec % 2, a, :], g, t * P, P),
                                perm_view(ps_t[:, a * P:(a + 1) * P], g, P), gains[:, a, g:g + 1],
                                perm_dest(qk_hi[:, sec % 2, a, :].bitcast(F32), g, t * P, P), ALU.mult, ALU.subtract)
                    if st >= 1:
                        slot = (TT * (st - 1) + j) % 3
                        ins = dve.tensor_tensor(v_lo[:, slot, :], ps_t[:, 2 * P:3 * P], v_hi[:, slot, :].bitcast(F32),
                                                ALU.subtract)
                    ins.then_inc(turn_lo, 1)
                if has_unit(st, j, 1):
                    sec, u = unit(st, j, 1)
                    b0 = 0 if has_prev(sec % NG, u) else 1
                    dve.wait_ge(p_hi_done, U)
                    dve.tensor_tensor(pT_lo[:, b0:2, :], ps_p[:].rearrange("p (b c) -> p b c", b=2)[:, b0:2, :],
                                      pT_hi[:, b0:2, :].bitcast(F32), ALU.subtract).then_inc(p_lo_done, 1)
                if st < SECTIONS:
                    dve.wait_ge(rs_done, T + 1)
                    if TT * st + j >= 2:
                        dve.wait_ge(turned, T - 1)
                    dve.tensor_tensor(qkn[:, j % 2, :].rearrange("p (h e) -> p h e", e=HD),
                                      ps_qk[j % 2][:, 0:2 * P].rearrange("p (h e) -> p h e", e=HD),
                                      rs[:].rearrange("p (h o) -> p h o", o=1).to_broadcast([P, 4, HD]), ALU.mult)\
                        .then_inc(qkn_done, 1)
                merge_step(i, st, j)

            def merge_step(i, st, j):
                if st >= 4 and (st - 4) % NG == 0:
                    pair = (st - 4) // NG + 2 * i
                    base = 10 * pair
                    if j == 1:
                        dve.wait_ge(exp_done, TT * (st + 6 * i) - TT)
                        for half in range(2):
                            dve.tensor_copy(compact[:, 2, :, :, half:16:2],
                                            stat[64 * half:64 * half + 64, (st - 2) % 2, :]
                                            .rearrange("p (s h u) -> p s h u", s=2, h=2)).then_inc(merge, 1)
                    m = [compact[:, 0, 0], compact[:, 1, 0].rearrange("p h (r c) -> p h c r", r=4), compact[:, 2, 0]]
                    d = [compact[:, 0, 1], compact[:, 1, 1].rearrange("p h (r c) -> p h c r", r=4), compact[:, 2, 1]]
                    nat = lambda ap, g: ap.rearrange("p h (c r) -> p h c r", r=4) if g == 1 else ap
                    if j == 2:
                        dve.wait_ge(compact_in[0], 64 * pair + 64)
                        dve.wait_ge(compact_in[1], 64 * pair + 64)
                        dve.wait_ge(merge, base + 2)
                        dve.tensor_tensor(top[:], m[0], m[2], ALU.max).then_inc(merge, 1)
                        dve.wait_ge(merge, base + 3)
                        dve.tensor_tensor(nat(top[:], 1), nat(top[:], 1), m[1], ALU.max).then_inc(merge, 1)
                        dve.wait_ge(merge, base + 4)
                        for g in range(NG):
                            ins = dve.tensor_tensor(nat(diff[:, g], g), m[g], nat(top[:], g), ALU.subtract)
                        ins.then_inc(diff_done, 1)
                    if j == 4:
                        dve.wait_ge(grown_done, pair + 1)
                        for g in range(NG):
                            dve.tensor_tensor(nat(part[:, g], g), nat(grown[:, g], g), d[g], ALU.mult).then_inc(merge, 1)
                        dve.wait_ge(merge, base + 7)
                        dve.tensor_tensor(den[:], part[:, 0], part[:, 1], ALU.add).then_inc(merge, 1)
                        dve.wait_ge(merge, base + 8)
                        dve.tensor_tensor(den[:], den[:], part[:, 2], ALU.add).then_inc(merge, 1)
                        dve.wait_ge(merge, base + 9)
                        dve.reciprocal(den[:], den[:]).then_inc(merge, 1)
                        dve.wait_ge(merge, base + 10)
                        for g in range(NG):
                            ins = dve.tensor_tensor(share[:, g], grown[:, g], den[:], ALU.mult)
                        ins.then_inc(share_done, 1)
                    if j == 7:
                        o0 = o_raw[0][:, ((st - 4) // NG) % 2, :]
                        dve.wait_ge(wbc_in[0], 64 * pair + 32)
                        dve.wait_ge(o_done, TT * (st + 6 * i) - TT)
                        dve.tensor_tensor(o0, o0, w_bc[:, 0, :], ALU.mult).then_inc(y_step, 1)
                if st >= 5 and (st - 5) % NG == 0:
                    pair = (st - 5) // NG + 2 * i
                    o0 = o_raw[0][:, ((st - 5) // NG) % 2, :]
                    if j == 1:
                        dve.wait_ge(wbc_in[1], 32 * pair + 32)
                        w = split_tokens(w_bc[:, 1, :], 1)
                        dve.tensor_tensor(w, w, natural_view(o_raw[1][:, 0, :], 1), ALU.mult).then_inc(y_step, 1)
                    if j == 2:
                        dve.wait_ge(y_step, 5 * pair + 2)
                        dve.tensor_tensor(o0, o0, w_bc[:, 1, :], ALU.add).then_inc(y_step, 1)
                    if j == 3:
                        dve.wait_ge(wbc_in[0], 64 * pair + 64)
                        w = split_tokens(w_bc[:, 0, :], 2)
                        dve.tensor_tensor(w, w, natural_view(o_raw[2][:, 0, :], 2), ALU.mult).then_inc(y_step, 1)
                    if j == 4:
                        dve.wait_ge(y_step, 5 * pair + 4)
                        dve.tensor_tensor(o0, o0, w_bc[:, 0, :], ALU.add).then_inc(y_step, 1)

            dve.wait_ge(set_done, 2)
            run_supersteps(dve, step)

        @block.gpsimd
        def _(pool):
            def lo_part(slot, par, k):
                pool.tensor_tensor(w_lo[:, par, k, :], raw[:, slot, :], w_hi[:, par, k, :].bitcast(F32),
                                   ALU.subtract).then_inc(w_lo_done, 1)

            pool.memset(minus_half[:], -0.5).then_inc(half_set, 1)
            for k in range(KT):
                pool.wait_ge(w_hi_done, k + 1)
                lo_part(k % 4, 0, k)
            pool.wait_ge(half_set, 1)

            def step(i, st, j):
                N = st + 6 * i
                T = TT * N + j
                if st + 1 < SECTIONS:
                    pool.wait_ge(w_hi_done, T + TT + 1)
                    lo_part(j % 4, (st + 1) % 2, j)
                if st < SECTIONS:
                    pool.wait_ge(var_done, T + 1)
                    if TT * st + j >= 1:
                        pool.wait_ge(qkn_done, T)
                    pool.tensor_tensor(rs[:], var[:], minus_half[:], ALU.pow).then_inc(rs_done, 1)

            run_supersteps(pool, step)



RAW_SLOTS = 4


def project_phase(nc, name, xT, w_pieces, yT, yT_dram, x_dram):
    with ExitStack() as ctx:
        sb = lambda n, s, d=F32: ctx.enter_context(nc.sbuf_tensor(f"{name}_{n}", s, d))
        sem = ctx.enter_context(phase_semaphores(nc, f"{name}_"))
        raw = sb("raw", [P, RAW_SLOTS, DM])
        w_hi = sb("w_hi", [P, 2, KT, P], F32R)
        w_lo = sb("w_lo", [P, 2, KT, P], F32R)
        yT_hi = sb("yT_hi", [P, KT, SEQ], F32R)
        yT_lo = sb("yT_lo", [P, KT, SEQ], F32R)
        y_raw = sb("y_raw", [P, 2, SEQ]) if yT is None else None
        ps = [ctx.enter_context(nc.psum_tensor(f"{name}_ps{i}", [P, HALF], F32)) for i in range(8)]
        raw_in = [sem(f"raw_in{i}") for i in range(RAW_SLOTS)]
        y_in = [sem(f"y_in{i}") for i in range(2)]
        x_in = sem("x_in")
        w_hi_done, w_lo_done, y_hi_done, y_lo_done = sem("w_hi_done"), sem("w_lo_done"), sem("y_hi_done"), sem("y_lo_done")
        product, x_added = sem("product"), sem("x_added")
        load = yT is None

        def y_tile(k):
            return y_raw[:, k % 2, :] if load else yT[:, k, :]

        block = ctx.enter_context(nc.Block())

        @block.sync
        def _(sp):
            for k in range(KT):
                if k < RAW_SLOTS:
                    sp.dma_start(raw[:, k, :], w_pieces[k]).then_inc(raw_in[k], 16)
                if load:
                    if k >= 2:
                        sp.wait_ge(y_lo_done, k - 1)
                    sp.dma_start(y_raw[:, k % 2, :], yT_dram[k]).then_inc(y_in[k % 2], 16)
            if load:
                sp.dma_start(xT[:], x_dram.rearrange("(k p) t -> p k t", p=P)).then_inc(x_in, 16)
            for n in range(RAW_SLOTS, KT):
                sp.wait_ge(w_lo_done, n - RAW_SLOTS + 1)
                sp.dma_start(raw[:, n % RAW_SLOTS, :], w_pieces[n]).then_inc(raw_in[n % RAW_SLOTS], 16)

        @block.scalar
        def _(act):
            for n in range(KT):
                if load:
                    act.wait_ge(y_in[n % 2], 16 * (n // 2 + 1))
                act.copy(yT_hi[:, n, :], y_tile(n)).then_inc(y_hi_done, 1)
                if n >= 1:
                    continue
                act.wait_ge(raw_in[0], 16)
                act.copy(w_hi[:, 0].rearrange("p k c -> p (k c)"), raw[:, 0, :]).then_inc(w_hi_done, 1)
            for n in range(1, KT):
                act.wait_ge(raw_in[n % RAW_SLOTS], 16 * (n // RAW_SLOTS + 1))
                if n >= 2:
                    act.wait_ge(product, 2 * (n - 1))
                act.copy(w_hi[:, n % 2].rearrange("p k c -> p (k c)"), raw[:, n % RAW_SLOTS, :]).then_inc(w_hi_done, 1)

        @block.gpsimd
        def _(pool):
            for n in range(KT):
                pool.wait_ge(w_hi_done, n + 1)
                pool.tensor_tensor(w_lo[:, n % 2].rearrange("p k c -> p (k c)"), raw[:, n % RAW_SLOTS, :],
                                   w_hi[:, n % 2].rearrange("p k c -> p (k c)").bitcast(F32),
                                   ALU.subtract).then_inc(w_lo_done, 1)

        @block.tensor
        def _(pe):
            for n in range(KT):
                pe.wait_ge(w_lo_done, n + 1)
                for half in range(2):
                    if n >= 4:
                        pe.wait_ge(x_added, 2 * (n - 4) + half + 1)
                    cols = slice(half * HALF, (half + 1) * HALF)
                    for k in range(KT):
                        if n == 0:
                            pe.wait_ge(y_lo_done, k + 1)
                        mm = split_matmul(pe, ps[(2 * n + half) % 8][:], w_hi[:, n % 2, k, :], w_lo[:, n % 2, k, :],
                                          yT_hi[:, k, cols], yT_lo[:, k, cols], k == 0, k == KT - 1)
                    mm.then_inc(product, 1)

        @block.vector
        def _(dve):
            for k in range(KT):
                dve.wait_ge(y_hi_done, k + 1)
                dve.tensor_tensor(yT_lo[:, k, :], y_tile(k), yT_hi[:, k, :].bitcast(F32), ALU.subtract).then_inc(y_lo_done, 1)
            if load:
                dve.wait_ge(x_in, 16)
            for n in range(KT):
                for half in range(2):
                    cols = slice(half * HALF, (half + 1) * HALF)
                    dve.wait_ge(product, 2 * n + half + 1)
                    dve.tensor_tensor(xT[:, n, cols], xT[:, n, cols], ps[(2 * n + half) % 8][:],
                                      ALU.add).then_inc(x_added, 1)
            dve.wait_ge(x_added, 2 * KT)


def mlp_phase(nc, name, xT, w1_pieces, w2_pieces, hT_hi, hT_lo, out_dram):
    with ExitStack() as ctx:
        sb = lambda n, s, d=F32: ctx.enter_context(nc.sbuf_tensor(f"{name}_{n}", s, d))
        sem = ctx.enter_context(phase_semaphores(nc, f"{name}_"))
        PIECES = 2 * KT
        raw = sb("raw", [P, RAW_SLOTS, DM])
        w_hi = sb("w_hi", [P, 2, KT, P], F32R)
        w_lo = sb("w_lo", [P, 2, KT, P], F32R)
        hid_hi = sb("hid_hi", [P, KT, SEQ], F32R)
        hid_lo = sb("hid_lo", [P, KT, SEQ], F32R)
        positive = sb("positive", [P, 2, HALF])
        squared = sb("squared", [P, HALF])
        ps = [ctx.enter_context(nc.psum_tensor(f"{name}_ps{i}", [P, HALF], F32)) for i in range(8)]
        raw_in = [sem(f"raw_in{i}") for i in range(RAW_SLOTS)]
        w_hi_done, w_lo_done, product = sem("w_hi_done"), sem("w_lo_done"), sem("product")
        relu_done, square_done, hid_hi_done, hid_lo_done = sem("relu_done"), sem("square_done"), sem("hid_hi_done"), sem("hid_lo_done")
        x_added, stored = sem("x_added"), sem("stored")
        block = ctx.enter_context(nc.Block())

        def run_chunks(eng, chunk):
            chunk(0, True)
            with eng.Fori(1, FCH) as c:
                chunk(c, False)

        @block.sync
        def _(sp):
            def piece(c, q):
                return w1_pieces[c, q] if q < KT else w2_pieces[c, q - KT]

            def load(c, q):
                sp.dma_start(raw[:, q % RAW_SLOTS, :], piece(c, q)).then_inc(raw_in[q % RAW_SLOTS], 16)

            def chunk(c, first):
                for q in range(PIECES):
                    if not first or q >= RAW_SLOTS:
                        sp.wait_ge(w_lo_done, PIECES * c + q - RAW_SLOTS + 1)
                    load(c, q)

            run_chunks(sp, chunk)
            if out_dram is not None:
                for d in range(KT):
                    sp.wait_ge(x_added, 2 * KT * (FCH - 1) + 2 * d + 2)
                    sp.dma_start(out_dram[d], xT[:, d, :]).then_inc(stored, 16)
                sp.wait_ge(stored, 16 * KT)

        @block.scalar
        def _(act):
            def hi_part(c, q, first):
                n = PIECES * c + q
                act.wait_ge(raw_in[q % RAW_SLOTS], 16 * (PIECES // RAW_SLOTS) * c + 16 * (q // RAW_SLOTS + 1))
                if not first or q >= 2:
                    act.wait_ge(product, 2 * n - 2)
                act.copy(w_hi[:, q % 2].rearrange("p k c -> p (k c)"), raw[:, q % RAW_SLOTS, :]).then_inc(w_hi_done, 1)

            def chunk(c, first):
                for q in range(PIECES):
                    if q == 0 and first:
                        hi_part(c, 0, True)
                    if q + 1 < PIECES:
                        hi_part(c, q + 1, first)
                    if q < KT:
                        for half in range(2):
                            m = 2 * KT * c + 2 * q + half
                            act.wait_ge(product, 2 * PIECES * c + 2 * q + half + 1)
                            if not first or q >= 1:
                                act.wait_ge(square_done, m - 1)
                            act.activation(positive[:, half, :], ps[(2 * q + half) % 8][:], ACT.Relu).then_inc(relu_done, 1)
                            act.wait_ge(relu_done, m + 1)
                            act.activation(hid_hi[:, q, half * HALF:(half + 1) * HALF], positive[:, half, :],
                                           ACT.Square).then_inc(hid_hi_done, 1)

            def between(c):
                hi_part(c, 0, False)

            def looped(c, first):
                if not first:
                    between(c)
                chunk(c, first)

            run_chunks(act, looped)

        @block.gpsimd
        def _(pool):
            def chunk(c, first):
                for q in range(PIECES):
                    pool.wait_ge(w_hi_done, PIECES * c + q + 1)
                    pool.tensor_tensor(w_lo[:, q % 2].rearrange("p k c -> p (k c)"), raw[:, q % RAW_SLOTS, :],
                                       w_hi[:, q % 2].rearrange("p k c -> p (k c)").bitcast(F32),
                                       ALU.subtract).then_inc(w_lo_done, 1)

            run_chunks(pool, chunk)

        @block.tensor
        def _(pe):
            def chunk(c, first):
                for q in range(PIECES):
                    pe.wait_ge(w_lo_done, PIECES * c + q + 1)
                    src_hi, src_lo = (hT_hi, hT_lo) if q < KT else (hid_hi, hid_lo)
                    for half in range(2):
                        cols = slice(half * HALF, (half + 1) * HALF)
                        if q >= 4 and q - 4 < KT:
                            pe.wait_ge(relu_done, 2 * KT * c + 2 * (q - 4) + half + 1)
                        elif q >= 4:
                            pe.wait_ge(x_added, 2 * KT * c + 2 * (q - 4 - KT) + half + 1)
                        elif not first:
                            pe.wait_ge(x_added, 2 * KT * c + 2 * (q - 4) + half + 1)
                        for k in range(KT):
                            if q == KT:
                                pe.wait_ge(hid_lo_done, 2 * KT * c + 2 * k + half + 1)
                            mm = split_matmul(pe, ps[(2 * q + half) % 8][:], w_hi[:, q % 2, k, :], w_lo[:, q % 2, k, :],
                                              src_hi[:, k, cols], src_lo[:, k, cols], k == 0, k == KT - 1)
                        mm.then_inc(product, 1)

            run_chunks(pe, chunk)

        @block.vector
        def _(dve):
            def chunk(c, first):
                for q in range(PIECES):
                    for half in range(2):
                        cols = slice(half * HALF, (half + 1) * HALF)
                        m = 2 * KT * c + 2 * (q % KT) + half
                        if q < KT:
                            dve.wait_ge(relu_done, m + 1)
                            if not first or q > 0 or half > 0:
                                dve.wait_ge(hid_lo_done, m)
                            dve.tensor_tensor(squared[:], positive[:, half, :], positive[:, half, :],
                                              ALU.mult).then_inc(square_done, 1)
                            dve.wait_ge(square_done, m + 1)
                            dve.wait_ge(hid_hi_done, m + 1)
                            dve.tensor_tensor(hid_lo[:, q, cols], squared[:], hid_hi[:, q, cols].bitcast(F32),
                                              ALU.subtract).then_inc(hid_lo_done, 1)
                        else:
                            dve.wait_ge(product, 2 * PIECES * c + 2 * q + half + 1)
                            if not first:
                                dve.wait_ge(x_added, m - 2 * KT + 1)
                            dve.tensor_tensor(xT[:, q - KT, cols], xT[:, q - KT, cols], ps[(2 * q + half) % 8][:],
                                              ALU.add).then_inc(x_added, 1)

            run_chunks(dve, chunk)



CONV = 4
QK_PIECES = 2 * MH
VO_CHUNKS = 4
VO_PIECES = 4 * VO_CHUNKS
VW = DV + 1


def mlstm_in_phase(nc, ident, qk_pieces, vo_pieces, gate_w, conv_w, conv_b, out_gain, hT_hi, hT_lo, qk, v1, gates, og_dram):
    with ExitStack() as ctx:
        sb = lambda n, s, d=F32: ctx.enter_context(nc.sbuf_tensor(f"mi_{n}", s, d))
        sem = ctx.enter_context(phase_semaphores(nc, "mi_"))
        raw = sb("raw", [P, 2, DM])
        w_hi = sb("w_hi", [P, 2, DM], F32R)
        w_lo = sb("w_lo", [P, 2, DM], F32R)
        g_raw = sb("g_raw", [P, KT, 2 * MH])
        g_hi = sb("g_hi", [P, KT, 2 * MH], F32R)
        g_lo = sb("g_lo", [P, KT, 2 * MH], F32R)
        padded = sb("padded", [P, 2, CONV - 1 + SEQ])
        acc = sb("acc", [P, SEQ])
        cw = sb("cw", [P, QK_PIECES, CONV])
        cb = sb("cb", [P, QK_PIECES])
        gain = sb("gain", [P, DM])
        sig = sb("sig", [P, 2, HALF])
        gT = sig[0:2 * MH].rearrange("p a c -> p (a c)")
        ps = [ctx.enter_context(nc.psum_tensor(f"mi_ps{i}", [P, HALF], F32)) for i in range(8)]
        raw_in = [sem(f"raw_in{i}") for i in range(2)]
        small_in, zeroed = sem("small_in"), sem("zeroed")
        w_hi_done, w_lo_done, g_hi_done, g_lo_done = sem("w_hi_done"), sem("w_lo_done"), sem("g_hi_done"), sem("g_lo_done")
        product, copied, conved, silu_done, scaled = sem("product"), sem("copied"), sem("conved"), sem("silu_done"), sem("scaled")
        gate_mm, gT_done, gates_turned = sem("gate_mm"), sem("gT_done"), sem("gates_turned")
        gates_done, tile_mm = sem("gates_done"), sem("tile_mm")
        v_done, sig_done, gained = sem("v_done"), sem("sig_done"), sem("gained")
        og_out = [sem(f"og_out{i}") for i in range(2)]
        block = ctx.enter_context(nc.Block())
        NP = QK_PIECES + VO_PIECES
        TILES_V = TT * VO_CHUNKS // 2

        @block.sync
        def _(sp):
            def store(tiles):
                for m in tiles:
                    c, t = divmod(m, TT)
                    sp.wait_ge(gained, m + 1)
                    sp.dma_start(og_dram[t, :, c * HALF:(c + 1) * HALF], sig[:, m % 2, :])\
                        .then_inc(og_out[m % 2], 16)

            sp.dma_start(cw[:], conv_w).then_inc(small_in, 16)
            sp.dma_start(cb[:], conv_b).then_inc(small_in, 16)
            sp.dma_start(gain[:], out_gain.to_broadcast([P, DM])).then_inc(small_in, 16)
            sp.dma_start(g_raw[:], gate_w).then_inc(small_in, 16)
            for n in range(NP):
                if n >= 2:
                    sp.wait_ge(w_lo_done, n - 1)
                sp.dma_start(raw[:, n % 2, :], qk_pieces[n] if n < QK_PIECES else vo_pieces[n - QK_PIECES])\
                    .then_inc(raw_in[n % 2], 16)
                if n == NP - 2:
                    store(range(TT))
            store(range(TT, TILES_V))
            for i in range(2):
                sp.wait_ge(og_out[i], 16 * TILES_V // 2)

        @block.gpsimd
        def _(pool):
            pool.memset(padded[:, :, 0:CONV - 1], 0.0).then_inc(zeroed, 1)
            pool.memset(v1[:, :, :, DV:VW], 1.0).then_inc(zeroed, 1)
            pool.wait_ge(g_hi_done, 1)
            pool.tensor_tensor(g_lo[:], g_raw[:], g_hi[:].bitcast(F32), ALU.subtract).then_inc(g_lo_done, 1)
            for n in range(NP):
                pool.wait_ge(w_hi_done, n + 1)
                pool.tensor_tensor(w_lo[:, n % 2, :], raw[:, n % 2, :], w_hi[:, n % 2, :].bitcast(F32),
                                   ALU.subtract).then_inc(w_lo_done, 1)

        @block.scalar
        def _(act):
            def hi_part(n):
                act.wait_ge(raw_in[n % 2], 16 * (n // 2 + 1))
                last = n - 2 - QK_PIECES
                if last >= 0 and last % 4 == 3:
                    act.wait_ge(tile_mm, TT * (last // 4 + 1))
                elif last >= 0:
                    act.wait_ge(product, QK_PIECES + 3 * (last // 4) + last % 4 + 1)
                elif n >= 2:
                    act.wait_ge(product, n - 1)
                act.copy(w_hi[:, n % 2, :], raw[:, n % 2, :]).then_inc(w_hi_done, 1)

            act.wait_ge(small_in, 64)
            act.copy(g_hi[:], g_raw[:]).then_inc(g_hi_done, 1)
            hi_part(0)
            for n in range(QK_PIECES):
                hi_part(n + 1)
                if n == 7:
                    act.wait_ge(gate_mm, 1)
                    for half in range(2):
                        act.copy(gT[:, half * HALF:(half + 1) * HALF], ps[half][0:2 * MH, :]).then_inc(gT_done, 1)
                act.wait_ge(product, n + 1)
                if n >= 2:
                    act.wait_ge(conved, CONV * (n - 1))
                for half in range(2):
                    c0 = CONV - 1 + half * HALF
                    act.copy(padded[:, n % 2, c0:c0 + HALF], ps[(2 * n + half) % 8][:]).then_inc(copied, 1)
                act.wait_ge(conved, CONV * (n + 1))
                act.activation(qk[:, n, :], acc[:], ACT.Silu, bias=cb[:, n:n + 1]).then_inc(silu_done, 1)
            for n in range(VO_PIECES):
                if n + 1 < VO_PIECES:
                    hi_part(QK_PIECES + n + 1)
                c = n // 4
                if n % 4 == 3 and c >= VO_CHUNKS // 2:
                    for t in range(TT):
                        m = TT * (c - VO_CHUNKS // 2) + t
                        act.wait_ge(tile_mm, TT * c + t + 1)
                        if m >= 2:
                            act.wait_ge(og_out[m % 2], 16 * (m // 2))
                        act.activation(sig[:, m % 2, :], ps[t][:], ACT.Sigmoid).then_inc(sig_done, 1)

        @block.vector
        def _(dve):
            dve.wait_ge(small_in, 64)
            dve.wait_ge(zeroed, 2)
            for n in range(QK_PIECES):
                src = padded[:, n % 2, :]
                dve.wait_ge(copied, 2 * n + 2)
                if n >= 1:
                    dve.wait_ge(silu_done, n)
                dve.tensor_scalar(acc[:], src[:, 0:SEQ], cw[:, n, 0:1], None, ALU.mult).then_inc(conved, 1)
                for w in range(1, CONV):
                    dve.wait_ge(conved, CONV * n + w)
                    dve.scalar_tensor_tensor(acc[:], src[:, w:w + SEQ], cw[:, n, w:w + 1], acc[:],
                                             ALU.mult, ALU.add).then_inc(conved, 1)
                if 1 <= n <= MH:
                    dve.wait_ge(silu_done, n)
                    dve.tensor_scalar(qk[:, n - 1, :], qk[:, n - 1, :], DK ** -0.5, None, ALU.mult).then_inc(scaled, 1)
            dve.wait_ge(gates_turned, 1)
            dve.tensor_copy(gates[:], ps[0][:, 0:TT * 2 * MH].rearrange("p (t g) -> p t g", g=2 * MH)).then_inc(gates_done, 1)
            for m in range(TILES_V):
                c, t = divmod(m, TT)
                dve.wait_ge(tile_mm, m + 1)
                dve.tensor_copy(v1[:, t, 2 * c:2 * c + 2, 0:DV],
                                ps[t][:].rearrange("p (h d) -> p h d", d=DV)).then_inc(v_done, 1)
            for m in range(TILES_V):
                c, t = divmod(m, TT)
                dve.wait_ge(sig_done, m + 1)
                dve.tensor_tensor(sig[:, m % 2, :], sig[:, m % 2, :], gain[:, c * HALF:(c + 1) * HALF],
                                  ALU.mult).then_inc(gained, 1)
            dve.wait_ge(v_done, TILES_V)

        @block.tensor
        def _(pe):
            for n in range(QK_PIECES):
                pe.wait_ge(w_lo_done, n + 1)
                if n >= 4:
                    pe.wait_ge(copied, 2 * (n - 4) + 2)
                for half in range(2):
                    cols = slice(half * HALF, (half + 1) * HALF)
                    for k in range(KT):
                        rows = slice(k * P, (k + 1) * P)
                        mm = split_matmul(pe, ps[(2 * n + half) % 8][:], w_hi[:, n % 2, rows], w_lo[:, n % 2, rows],
                                          hT_hi[:, k, cols], hT_lo[:, k, cols], k == 0, k == KT - 1)
                mm.then_inc(product, 1)
                if n == 5:
                    pe.wait_ge(g_lo_done, 1)
                    pe.wait_ge(copied, 2 * 5)
                    for half in range(2):
                        cols = slice(half * HALF, (half + 1) * HALF)
                        for k in range(KT):
                            mm = split_matmul(pe, ps[half][0:2 * MH, :], g_hi[:, k, :], g_lo[:, k, :],
                                              hT_hi[:, k, cols], hT_lo[:, k, cols], k == 0, k == KT - 1)
                    mm.then_inc(gate_mm, 1)
            pe.wait_ge(gT_done, 2)
            for t in range(TT):
                mm = pe.transpose(ps[0][:, t * 2 * MH:(t + 1) * 2 * MH], gT[:, t * P:(t + 1) * P],
                                  ident[0:2 * MH, 0:2 * MH])
            mm.then_inc(gates_turned, 1)
            for n in range(VO_PIECES):
                c = n // 4
                pe.wait_ge(w_lo_done, QK_PIECES + n + 1)
                for kk in range(2):
                    k = 2 * (n % 4) + kk
                    cols = slice(kk * HALF, (kk + 1) * HALF)
                    for t in range(TT):
                        if k == 0:
                            if c == 0:
                                pe.wait_ge(gates_done, 1)
                                pe.wait_ge(copied, 2 * QK_PIECES)
                            elif c <= VO_CHUNKS // 2:
                                pe.wait_ge(v_done, TT * (c - 1) + t + 1)
                            else:
                                pe.wait_ge(sig_done, TT * (c - 1 - VO_CHUNKS // 2) + t + 1)
                        mm = split_matmul(pe, ps[t][:], hT_hi[:, k, t * P:(t + 1) * P], hT_lo[:, k, t * P:(t + 1) * P],
                                          w_hi[:, (QK_PIECES + n) % 2, cols], w_lo[:, (QK_PIECES + n) % 2, cols],
                                          k == 0, k == KT - 1)
                        if k == KT - 1:
                            mm.then_inc(tile_mm, 1)
                if n % 4 != 3:
                    mm.then_inc(product, 1)


def mlstm_cell_phase(nc, ones, ident, gates, gate_bias, qk, v1, og_dram, yT):
    with ExitStack() as ctx:
        sb = lambda n, s, d=F32: ctx.enter_context(nc.sbuf_tensor(f"mc_{n}", s, d))
        psum = lambda n, s: ctx.enter_context(nc.psum_tensor(f"mc_{n}", s, F32))
        sem = ctx.enter_context(phase_semaphores(nc, "mc_"))
        CH = CHUNKS * MH
        gb = sb("gb", [P, 2 * MH])
        upto = sb("upto", [P, P])
        mask = sb("mask", [P, MH, P])
        size = sb("size", [P, CHUNKS, MH])
        low = sb("low", [P, CHUNKS, MH])
        log_f = sb("log_f", [P, CHUNKS, MH])
        b_sum = sb("b_sum", [P, CHUNKS, MH])
        b_last = sb("b_last", [P, CHUNKS, MH])
        a = sb("a", [P, CHUNKS, MH])
        a_row = sb("a_row", [P, CHUNKS, MH, P])
        a_max = sb("a_max", [P, CHUNKS, MH])
        run_max = sb("run_max", [P, CHUNKS, MH])
        m_before = sb("m_before", [P, CHUNKS + 1, MH])
        A = sb("A", [P, CHUNKS, MH])
        neg_A = sb("neg_A", [P, CHUNKS, MH])
        inter = sb("inter", [P, CHUNKS, MH])
        floor = sb("floor", [P, CHUNKS, MH])
        decay = sb("decay", [P, CHUNKS, MH])
        key_w = sb("key_w", [P, CHUNKS, MH])
        state = sb("state", [P, MH, VW])
        E = sb("E", [P, 2, MH, P])
        spread = E
        W = sb("W", [P, MH, P])
        WT = sb("WT", [P, MH, P])
        kw = sb("kw", [P, 2, MH, P])
        carried = sb("carried", [P, 2, VW])
        num = sb("num", [P, 2, MH, VW])
        og = sb("og", [P, 2, DM])
        junk = sb("junk", [P, DV])
        r_den = sb("r_den", [P, MH])
        sums = sb("sums", [P, MH])
        rms = sb("rms", [P, MH])
        factor = sb("factor", [P, MH])
        minus_half = sb("minus_half", [P, MH])
        y = sb("y", [P, DM])
        ps_s = psum("ps_s", [P, HALF])
        ps_k = psum("ps_k", [P, HALF])
        ps_w = psum("ps_w", [P, HALF])
        ps_in = [psum(f"ps_in{i}", [P, HALF]) for i in range(2)]
        ps_st = [psum(f"ps_st{i}", [P, HALF]) for i in range(2)]
        ps_d = psum("ps_d", [P, HALF])
        gb_in = sem("gb_in")
        og_in = [sem(f"og_in{i}") for i in range(2)]
        built, prep, lut, cums = sem("built"), sem("prep"), sem("lut"), sem("cums")
        spread_done, rows_mm, row_read = sem("spread_done"), sem("rows_mm"), sem("row_read")
        chain, ready, exps = sem("chain"), sem("ready"), sem("exps")
        E_done, scored, k_turned, W_done, W_turned = sem("E_done"), sem("scored"), sem("k_turned"), sem("W_done"), sem("W_turned")
        WT_done, kw_done, within, from_state, grown = sem("WT_done"), sem("kw_done"), sem("within"), sem("from_state"), sem("grown")
        carried_done, num_done, state_done = sem("carried_done"), sem("num_done"), sem("state_done")
        tail, summed, root = sem("tail"), sem("summed"), sem("root")
        y_done, y_turned, y_kept = sem("y_done"), sem("y_turned"), sem("y_kept")
        block = ctx.enter_context(nc.Block())
        flat = lambda t: t[:].rearrange("p c h -> p (c h)")

        @block.sync
        def _(sp):
            sp.dma_start(gb[:], gate_bias.to_broadcast([P, 2 * MH])).then_inc(gb_in, 16)
            for c in range(CHUNKS):
                if c >= 2:
                    sp.wait_ge(og_in[c % 2], 16 * (c // 2))
                    sp.wait_ge(y_done, MH * (c - 1))
                sp.dma_start(og[:, c % 2, :], og_dram[c]).then_inc(og_in[c % 2], 16)

        @block.gpsimd
        def _(pool):
            pool.memset(minus_half[:], -0.5).then_inc(built, 1)
            pool.memset(upto[:], 1.0).then_inc(built, 1)
            pool.memset(mask[:], 0.0).then_inc(built, 1)
            pool.memset(m_before[:, 0, :], 0.0).then_inc(built, 1)
            pool.memset(state[:], 0.0).then_inc(built, 1)
            pool.memset(sums[:], 0.0).then_inc(built, 1)
            pool.wait_ge(built, 6)
            pool.affine_select(out=upto[:], in_=upto[:], compare_op=ALU.is_ge, fill=0.0, base=0,
                               pattern=[[1, P]], channel_multiplier=-1).then_inc(built, 1)
            for h in range(MH):
                pool.affine_select(out=mask[:, h, :], in_=mask[:, h, :], compare_op=ALU.is_ge, fill=MASKED, base=0,
                                   pattern=[[-1, P]], channel_multiplier=1).then_inc(built, 1)
            for c in range(CHUNKS):
                pool.wait_ge(tail, 5 * c + 4)
                if c >= 1:
                    pool.wait_ge(tail, 5 * c)
                pool.tensor_tensor(rms[:], sums[:], minus_half[:], ALU.pow).then_inc(root, 1)

        @block.scalar
        def _(act):
            act.wait_ge(prep, 2)
            act.activation(size[:], size[:], ACT.Exp, scale=-1.0).then_inc(lut, 1)
            act.wait_ge(prep, 3)
            act.activation(size[:], size[:], ACT.Ln).then_inc(lut, 1)
            act.wait_ge(built, 11)
            act.wait_ge(ready, 1)
            act.activation(inter[:], inter[:], ACT.Exp).then_inc(exps, 1)
            act.activation(floor[:], floor[:], ACT.Exp, scale=-1.0).then_inc(exps, 1)
            act.activation(decay[:], decay[:], ACT.Exp).then_inc(exps, 1)
            act.activation(key_w[:], key_w[:], ACT.Exp).then_inc(exps, 1)

            def key_weights(c):
                if c >= 2:
                    act.wait_ge(W_done, c - 1)
                else:
                    act.wait_ge(rows_mm, CHUNKS)
                for h in range(MH):
                    act.activation(E[:, c % 2, h, :], a_row[:, c, h, :], ACT.Exp, bias=neg_A[:, c, h:h + 1])\
                       .then_inc(E_done, 1)

            def turned_weights(c):
                act.wait_ge(W_turned, c + 1)
                act.copy(WT[:], ps_w[:].rearrange("p (h s) -> p h s", h=MH)).then_inc(WT_done, 1)

            def carry(c, h):
                n = MH * c + h
                act.wait_ge(from_state, n + 1)
                if n >= 2:
                    act.wait_ge(num_done, n - 1)
                act.activation(carried[:, n % 2, :], ps_st[n % 2][:, 0:VW], ACT.Copy,
                               scale=inter[:, c, h:h + 1]).then_inc(carried_done, 1)

            def square_sums(c):
                act.wait_ge(tail, 5 * c + 3)
                for h in range(MH):
                    if h or c:
                        act.wait_ge(summed, MH * c + h)
                    act.activation(junk[:], num[:, c % 2, h, 0:DV], ACT.Square, scale=r_den[:, h:h + 1],
                                   accum_out=sums[:, h:h + 1]).then_inc(summed, 1)

            def keep_y(c, part):
                act.wait_ge(y_turned, 2 * c + part + 1)
                act.copy(yT[:, 4 * part:4 * part + 4, c * P:(c + 1) * P],
                         ps_w[:].rearrange("p (k t) -> p k t", k=4)).then_inc(y_kept, 1)

            key_weights(0)
            key_weights(1)
            turned_weights(0)
            for c in range(CHUNKS + 2):
                for part in range(2):
                    if c < CHUNKS:
                        carry(c, 2 * part)
                        carry(c, 2 * part + 1)
                    if part == 0 and 1 <= c <= CHUNKS:
                        square_sums(c - 1)
                    if c >= 2:
                        keep_y(c - 2, part)
                if c + 2 < CHUNKS:
                    key_weights(c + 2)
                if c + 1 < CHUNKS:
                    turned_weights(c + 1)

        @block.vector
        def _(dve):
            def rows(c):
                dve.wait_ge(rows_mm, c + 1)
                bank = ps_in[c % 2][:].rearrange("p (h s) -> p h s", h=MH)
                dve.tensor_reduce(a_max[:, c, :], bank, AX.X, ALU.max)
                for h in range(MH):
                    ins = dve.tensor_tensor_reduce(a_row[:, c, h, :], bank[:, h, :], mask[:, h, :], 1.0, -3.0e38,
                                                   ALU.add, ALU.max, run_max[:, c, h:h + 1])
                ins.then_inc(row_read, 1)

            dve.wait_ge(gb_in, 16)
            gi, gf = gates[:, :, 0:MH], gates[:, :, MH:2 * MH]
            dve.tensor_tensor(gates[:], gates[:],
                              gb[:].rearrange("p (o g) -> p o g", o=1).to_broadcast([P, CHUNKS, 2 * MH]), ALU.add)\
                .then_inc(prep, 1)
            dve.wait_ge(prep, 1)
            dve.tensor_scalar(low[:], gf, 0.0, None, ALU.min)
            dve.scalar_tensor_tensor(size[:], gf, -1.0, gf, ALU.mult, ALU.max).then_inc(prep, 1)
            dve.wait_ge(lut, 1)
            dve.tensor_scalar(size[:], size[:], 1.0, None, ALU.add).then_inc(prep, 1)
            dve.wait_ge(lut, 2)
            dve.tensor_tensor(log_f[:], low[:], size[:], ALU.subtract).then_inc(prep, 1)
            dve.wait_ge(cums, 2)
            dve.tensor_copy(flat(b_sum), ps_s[:, 0:CH])
            dve.tensor_copy(flat(b_last), ps_k[:, 0:CH]).then_inc(prep, 1)
            dve.wait_ge(prep, 5)
            dve.tensor_tensor(a[:], gi, b_sum[:], ALU.subtract).then_inc(prep, 1)
            dve.wait_ge(prep, 6)
            dve.wait_ge(built, 11)
            for c in range(CHUNKS):
                if c >= 2:
                    dve.wait_ge(rows_mm, c - 1)
                dve.tensor_tensor(spread[:, c % 2], ident[:].rearrange("p (o s) -> p o s", o=1).to_broadcast([P, MH, P]),
                                  a[:, c, :].rearrange("p (h o) -> p h o", o=1).to_broadcast([P, MH, P]), ALU.mult)\
                    .then_inc(spread_done, 1)
                if c >= 1:
                    rows(c - 1)
            rows(CHUNKS - 1)
            n = 0
            for c in range(CHUNKS):
                if n:
                    dve.wait_ge(chain, n)
                dve.wait_ge(row_read, CHUNKS)
                dve.tensor_tensor(m_before[:, c + 1, :], m_before[:, c, :], a_max[:, c, :], ALU.max).then_inc(chain, 1)
                dve.wait_ge(chain, n + 1)
                dve.tensor_tensor(m_before[:, c + 1, :], m_before[:, c + 1, :], b_last[:, c, :], ALU.add).then_inc(chain, 1)
                n += 2
            dve.wait_ge(chain, n)
            before, after = m_before[:, 0:CHUNKS, :], m_before[:, 1:CHUNKS + 1, :]
            dve.tensor_tensor(A[:], before, run_max[:], ALU.max).then_inc(chain, 1)
            dve.tensor_tensor(decay[:], before, after, ALU.subtract).then_inc(chain, 1)
            dve.tensor_tensor(key_w[:], b_last[:], after, ALU.subtract).then_inc(chain, 1)
            dve.wait_ge(chain, n + 3)
            dve.tensor_scalar(neg_A[:], A[:], -1.0, None, ALU.mult)
            dve.tensor_tensor(inter[:], before, A[:], ALU.subtract)
            dve.tensor_tensor(floor[:], b_sum[:], A[:], ALU.add)
            dve.tensor_tensor(decay[:], decay[:], b_last[:], ALU.add)
            dve.tensor_tensor(key_w[:], key_w[:], a[:], ALU.add).then_inc(ready, 1)
            dve.wait_ge(exps, 4)

            def weigh_scores(c):
                dve.wait_ge(scored, c + 1)
                dve.wait_ge(E_done, MH * (c + 1))
                if c >= 1:
                    dve.wait_ge(W_turned, c)
                dve.tensor_tensor(W[:], ps_s[:].rearrange("p (h s) -> p h s", h=MH), E[:, c % 2], ALU.mult).then_inc(W_done, 1)

            def weigh_keys(c):
                dve.wait_ge(k_turned, c + 1)
                if c >= 2:
                    dve.wait_ge(grown, MH * (c - 1))
                dve.tensor_tensor(kw[:, c % 2], ps_k[:].rearrange("p (h s) -> p h s", h=MH),
                                  key_w[:, c, :].rearrange("p (h o) -> p h o", o=1).to_broadcast([P, MH, P]), ALU.mult)\
                    .then_inc(kw_done, 1)

            def head(c, h):
                n = MH * c + h
                dve.wait_ge(carried_done, n + 1)
                dve.wait_ge(within, n + 1)
                if c >= 2:
                    dve.wait_ge(y_done, n - 2 * MH + 1)
                dve.tensor_tensor(num[:, c % 2, h, :], ps_in[n % 2][:, 0:VW], carried[:, n % 2, :], ALU.add)\
                    .then_inc(num_done, 1)
                dve.wait_ge(grown, n + 1)
                if c >= 1:
                    dve.wait_ge(state_done, n - MH + 1)
                dve.scalar_tensor_tensor(state[:, h, :], state[:, h, :], decay[:, c, h:h + 1], ps_d[:, 0:VW],
                                         ALU.mult, ALU.add).then_inc(state_done, 1)

            def denominators(c):
                dve.wait_ge(num_done, MH * (c + 1))
                if c >= 1:
                    dve.wait_ge(tail, 5 * c)
                den = num[:, c % 2, :, DV]
                dve.scalar_tensor_tensor(r_den[:], den, -1.0, floor[:, c, :], ALU.mult, ALU.max).then_inc(tail, 1)
                dve.wait_ge(tail, 5 * c + 1)
                dve.tensor_tensor(r_den[:], r_den[:], den, ALU.max).then_inc(tail, 1)
                dve.wait_ge(tail, 5 * c + 2)
                dve.reciprocal(r_den[:], r_den[:]).then_inc(tail, 1)

            def mean_squares(c):
                dve.wait_ge(summed, MH * (c + 1))
                dve.tensor_scalar(sums[:], sums[:], 1.0 / DV, EPS, ALU.mult, ALU.add).then_inc(tail, 1)

            def factors(c):
                dve.wait_ge(root, c + 1)
                if c >= 1:
                    dve.wait_ge(y_done, MH * c)
                dve.tensor_tensor(factor[:], r_den[:], rms[:], ALU.mult).then_inc(tail, 1)

            def outputs(c):
                dve.wait_ge(tail, 5 * c + 5)
                dve.wait_ge(og_in[c % 2], 16 * (c // 2 + 1))
                if c >= 1:
                    dve.wait_ge(y_turned, 2 * c)
                for h in range(MH):
                    dve.scalar_tensor_tensor(y[:, h * DV:(h + 1) * DV], num[:, c % 2, h, 0:DV], factor[:, h:h + 1],
                                             og[:, c % 2, h * DV:(h + 1) * DV], ALU.mult, ALU.mult).then_inc(y_done, 1)

            weigh_scores(0)
            weigh_keys(0)
            for c in range(CHUNKS + 1):
                for h in range(MH):
                    if c < CHUNKS:
                        head(c, h)
                    if h == 0 and c + 1 < CHUNKS:
                        weigh_scores(c + 1)
                    if h == 1 and c + 1 < CHUNKS:
                        weigh_keys(c + 1)
                    if h == 2 and c >= 1:
                        mean_squares(c - 1)
                if c >= 1:
                    factors(c - 1)
                if c < CHUNKS:
                    denominators(c)
                if c >= 1:
                    outputs(c - 1)

        @block.tensor
        def _(pe):
            pe.wait_ge(prep, 4)
            pe.wait_ge(built, 7)
            pe.matmul(ps_s[:, 0:CH], upto[:], flat(log_f), start=True, stop=True).then_inc(cums, 1)
            pe.matmul(ps_k[:, 0:CH], ones[:], flat(log_f), start=True, stop=True).then_inc(cums, 1)
            for c in range(CHUNKS):
                pe.wait_ge(spread_done, c + 1)
                if c >= 2:
                    pe.wait_ge(row_read, c - 1)
                pe.matmul(ps_in[c % 2][:], ones[:], spread[:, c % 2].rearrange("p h s -> p (h s)"),
                          start=True, stop=True).then_inc(rows_mm, 1)
            pe.wait_ge(prep, 5)
            pe.wait_ge(row_read, CHUNKS)

            def scores(c):
                cols = slice(c * P, (c + 1) * P)
                if c >= 1:
                    pe.wait_ge(W_done, c)
                for h in range(MH):
                    mm = pe.matmul(ps_s[:, h * P:(h + 1) * P], qk[:, h, cols], qk[:, MH + h, cols], start=True, stop=True)
                mm.then_inc(scored, 1)
                if c >= 1:
                    pe.wait_ge(kw_done, c)
                for h in range(MH):
                    mm = pe.transpose(ps_k[:, h * P:(h + 1) * P], qk[:, MH + h, cols], ident[:])
                mm.then_inc(k_turned, 1)

            def turn_weights(c):
                pe.wait_ge(W_done, c + 1)
                if c >= 1:
                    pe.wait_ge(WT_done, c)
                if c >= 3:
                    pe.wait_ge(y_kept, 2 * c - 4)
                for h in range(MH):
                    mm = pe.transpose(ps_w[:, h * P:(h + 1) * P], W[:, h, :], ident[:])
                mm.then_inc(W_turned, 1)

            def head(c, h):
                n = MH * c + h
                if n >= 2:
                    pe.wait_ge(carried_done, n - 1)
                if c >= 1:
                    pe.wait_ge(state_done, n - MH + 1)
                pe.matmul(ps_st[n % 2][:, 0:VW], qk[:, h, c * P:(c + 1) * P], state[:, h, :], start=True, stop=True)\
                    .then_inc(from_state, 1)
                pe.wait_ge(WT_done, c + 1)
                if n >= 2:
                    pe.wait_ge(num_done, n - 1)
                pe.matmul(ps_in[n % 2][:, 0:VW], WT[:, h, :], v1[:, c, h, :], start=True, stop=True).then_inc(within, 1)
                pe.wait_ge(kw_done, c + 1)
                if n >= 1:
                    pe.wait_ge(state_done, n)
                pe.matmul(ps_d[:, 0:VW], kw[:, c % 2, h, :], v1[:, c, h, :], start=True, stop=True).then_inc(grown, 1)

            def turn_y(c, part):
                pe.wait_ge(y_done, MH * c + 2 * part + 2)
                pe.wait_ge(WT_done, min(c + 3, CHUNKS))
                if c or part:
                    pe.wait_ge(y_kept, 2 * c + part)
                for j in range(4):
                    f = 4 * part + j
                    mm = pe.transpose(ps_w[:, j * P:(j + 1) * P], y[:, f * P:(f + 1) * P], ident[:])
                mm.then_inc(y_turned, 1)

            scores(0)
            turn_weights(0)
            for c in range(CHUNKS + 2):
                if c + 1 < CHUNKS:
                    scores(c + 1)
                for part in range(2):
                    if c < CHUNKS:
                        head(c, 2 * part)
                        head(c, 2 * part + 1)
                    if c >= 2:
                        turn_y(c - 2, part)
                if c + 1 < CHUNKS:
                    turn_weights(c + 1)


def mlstm_phases(nc, xT, ones, ident, norm_gain, qk_pieces, vo_pieces, gate_w, conv_w, conv_b, out_gain, gate_bias, keep):
    og_dram = nc.dram_tensor("og_dram", [TT, P, DM], F32, kind="Internal").ap()
    with ExitStack() as ctx:
        qk = ctx.enter_context(nc.sbuf_tensor("mlstm_qk", [P, QK_PIECES, SEQ], F32))
        v1 = ctx.enter_context(nc.sbuf_tensor("mlstm_v1", [P, TT, MH, VW], F32))
        gates = ctx.enter_context(nc.sbuf_tensor("mlstm_gates", [P, TT, 2 * MH], F32))
        with split_hidden(nc, "mlstm") as (hT_hi, hT_lo):
            norm_phase(nc, "norm_mlstm", xT, None, norm_gain, ones, hT_hi, hT_lo)
            mlstm_in_phase(nc, ident, qk_pieces, vo_pieces, gate_w, conv_w, conv_b, out_gain, hT_hi, hT_lo, qk, v1, gates, og_dram)
        yT = keep.enter_context(nc.sbuf_tensor("mlstm_yT", [P, KT, SEQ], F32, side="right"))
        mlstm_cell_phase(nc, ones, ident, gates, gate_bias, qk, v1, og_dram, yT)
    return yT


@contextmanager
def split_hidden(nc, name):
    with nc.sbuf_tensor(f"{name}_hT_hi", [P, KT, SEQ], F32R) as hi, nc.sbuf_tensor(f"{name}_hT_lo", [P, KT, SEQ], F32R) as lo:
        yield hi, lo


def trunk(nc, xT_in, mixer_gain, mlp_gain, rel_bias, onehot, wqkv, q_gain, k_gain, attn_wo, qk_pieces, vo_pieces,
          gate_w, gate_bias, conv_w, conv_b, out_gain, mlstm_wo, w1, w2, out):
    bias_dram = nc.dram_tensor("bias_dram", [NG, HEADS, BIAS_LEN], F32, kind="Internal").ap()
    yT_dram = nc.dram_tensor("yT_dram", [PAIRS, P, SEQ], F32, kind="Internal").ap()
    with ExitStack() as ctx:
        ones = ctx.enter_context(nc.sbuf_tensor("ones", [P, P], F32))
        ident = ctx.enter_context(nc.sbuf_tensor("ident", [P, P], F32))
        constants_phase(nc, ones, ident, rel_bias, onehot, bias_dram)
        with split_hidden(nc, "attn") as (hT_hi, hT_lo):
            with nc.sbuf_tensor("x_first", [P, KT, SEQ], F32) as x_first:
                norm_phase(nc, "norm_attn", x_first, xT_in, mixer_gain[0], ones, hT_hi, hT_lo)
            attention_phase(nc, ident, hT_hi, hT_lo, wqkv, q_gain, k_gain, bias_dram, yT_dram)
        xT = ctx.enter_context(nc.sbuf_tensor("xT", [P, KT, SEQ], F32, side="right"))
        project_phase(nc, "attn_out", xT, attn_wo, None, yT_dram, xT_in)
        with split_hidden(nc, "mlp0") as (hT_hi, hT_lo):
            norm_phase(nc, "norm_mlp0", xT, None, mlp_gain[0], ones, hT_hi, hT_lo)
            mlp_phase(nc, "mlp0", xT, w1[0], w2[0], hT_hi, hT_lo, None)
        with ExitStack() as keep:
            yT = mlstm_phases(nc, xT, ones, ident, mixer_gain[1], qk_pieces, vo_pieces, gate_w, conv_w, conv_b,
                              out_gain, gate_bias, keep)
            project_phase(nc, "mlstm_out", xT, mlstm_wo, yT, None, None)
        with split_hidden(nc, "mlp1") as (hT_hi, hT_lo):
            norm_phase(nc, "norm_mlp1", xT, None, mlp_gain[1], ones, hT_hi, hT_lo)
            mlp_phase(nc, "mlp1", xT, w1[1], w2[1], hT_hi, hT_lo, out)



def stationary_pieces(w):
    return np.ascontiguousarray(w.reshape(KT, P, KT, P).transpose(2, 1, 0, 3)).reshape(KT, P, DM)


def kernel(x, mixer_norm, mlp_norm, rel_bias, attn_w_in, attn_q_gain, attn_k_gain, attn_w_out, mlstm_w_in,
           mlstm_gate_bias, mlstm_conv_w, mlstm_conv_b, mlstm_out_gain, mlstm_w_out, mlp_w_in, mlp_w_out):
    import concourse.bacc as bacc
    from concourse.bass_utils import run_bass_kernel_spmd

    depth = mlp_w_in.shape[0]
    lay = np.ascontiguousarray
    w_in = mlstm_w_in[0]
    per_tile = lambda v: lay(v.reshape(-1, KT, P).transpose(0, 2, 1))
    arrays = {
        "xT_in": lay(x[0].T),
        "mixer_gain": per_tile(mixer_norm),
        "mlp_gain": per_tile(mlp_norm),
        "rel_bias": lay(rel_bias),
        "onehot": bias_onehot(),
        "wqkv": lay(attn_w_in[0].reshape(KT, P, 3, NG, PAIRS, P).transpose(4, 3, 0, 1, 2, 5)).reshape(SECTIONS * KT, P, 3 * P),
        "q_gain": lay(attn_q_gain[0].T),
        "k_gain": lay(attn_k_gain[0].T),
        "attn_wo": stationary_pieces(attn_w_out[0]),
        "qk_pieces": stationary_pieces(w_in[:, :DM]),
        "vo_pieces": lay(w_in[:, DM:3 * DM].reshape(4, 2, P, VO_CHUNKS, HALF).transpose(3, 0, 2, 1, 4)).reshape(VO_PIECES, P, DM),
        "gate_w": lay(w_in[:, 3 * DM:].reshape(KT, P, 2 * MH).transpose(1, 0, 2)),
        "gate_bias": lay(mlstm_gate_bias),
        "conv_w": lay(mlstm_conv_w[0].reshape(CONV, KT, P).transpose(2, 1, 0)),
        "conv_b": lay(mlstm_conv_b[0].reshape(KT, P).T),
        "out_gain": lay(mlstm_out_gain[0].reshape(1, DM)),
        "mlstm_wo": stationary_pieces(mlstm_w_out[0]),
        "w1": lay(mlp_w_in.reshape(depth, KT, P, FCH, KT, P).transpose(0, 3, 4, 2, 1, 5)).reshape(depth, FCH, KT, P, DM),
        "w2": lay(mlp_w_out.reshape(depth, FCH, KT, P, KT, P).transpose(0, 1, 4, 3, 2, 5)).reshape(depth, FCH, KT, P, DM),
    }
    nc = bacc.Bacc("TRN2", target_bir_lowering=False, num_devices=1)
    args = {n: nc.dram_tensor(f"in_{n}", a.shape, mybir.dt.from_np(a.dtype), kind="ExternalInput").ap()
            for n, a in arrays.items()}
    out = nc.dram_tensor("out_xT", [KT, P, SEQ], F32, kind="ExternalOutput").ap()
    trunk(nc, **args, out=out)
    r = run_bass_kernel_spmd(nc, [{f"in_{n}": a for n, a in arrays.items()}], core_ids=[0])
    return lay(r.results[0]["out_xT"].reshape(DM, SEQ).T).reshape(1, SEQ, DM)
```

```python
import math
from contextlib import ExitStack, contextmanager

import numpy as np

import concourse.bass as bass
from concourse import mybir

F32 = mybir.dt.float32
F32R = mybir.dt.float32r
ALU = mybir.AluOpType
ACT = mybir.ActivationFunctionType
AX = mybir.AxisListType

P = 128
DM = 1024
SEQ = 1024
KT = DM // P
TT = SEQ // P
HALF = 512
EPS = 1e-6

GROUPS = ((128, 1), (512, 4), (2048, 16))
NG = len(GROUPS)
HEADS = 16
HD = DM // HEADS
PAIRS = HEADS // 2
SECTIONS = PAIRS * NG
REL_BUCKETS = 32
REL_MAX = 2048
BIAS_LEN = 384
MASKED = -1.0e30

MH = 4
DK = 128
DV = 256
CHUNKS = SEQ // P

DFF = 4 * DM
FCH = DFF // DM


def bias_onehot():
    out = np.zeros((NG, REL_BUCKETS + 1, BIAS_LEN), np.float32)
    exact = REL_BUCKETS // 2
    for g, (window, dilation) in enumerate(GROUPS):
        band = window // dilation
        for x in range(BIAS_LEN):
            step = x - (P - 1)
            if step < 0 or step > band:
                out[g, REL_BUCKETS, x] = 1.0
                continue
            dist = step * dilation
            large = exact + int(np.float32(np.log(np.float32(max(dist, 1)) / np.float32(exact)))
                                / np.float32(math.log(REL_MAX / exact)) * np.float32(REL_BUCKETS - exact))
            out[g, dist if dist < exact else min(large, REL_BUCKETS - 1), x] = 1.0
    return out


def split_matmul(pe, out, a_hi, a_lo, b_hi, b_lo, first, last):
    pe.matmul(out, a_hi, b_hi, start=first, stop=False)
    pe.matmul(out, a_hi, b_lo, start=False, stop=False)
    return pe.matmul(out, a_lo, b_hi, start=False, stop=last)


def perm_view(ap, g, width):
    if g == 0:
        return ap
    return ap.rearrange("p (i r) -> p r i", r=GROUPS[g][1])


def perm_dest(buf, g, t0, width):
    if g == 0:
        return buf[:, t0:t0 + width]
    d = GROUPS[g][1]
    if g == 1:
        n, i0 = t0 // HALF, (t0 % HALF) // d
        return buf.rearrange("p (r n i) -> p r n i", r=d, n=2)[:, :, n, i0:i0 + width // d]
    return buf.rearrange("p (r i) -> p r i", r=d)[:, :, t0 // d:(t0 + width) // d]


def natural_view(buf, g):
    if g == 0:
        return buf
    if g == 1:
        return buf.rearrange("p (r n i) -> p n i r", r=4, n=2)
    return buf.rearrange("p (r i) -> p i r", r=16)


def split_tokens(ap, g):
    if g == 0:
        return ap
    if g == 1:
        return ap.rearrange("p (n i r) -> p n i r", n=2, r=4)
    return ap.rearrange("p (i r) -> p i r", r=16)


@contextmanager
def phase_semaphores(nc, prefix):
    made = []

    def sem(name):
        made.append(nc.alloc_semaphore(name=prefix + name))
        return made[-1]

    yield sem
    nc.clear_and_free_semaphores(made)
    nc.all_engine_barrier()



def tiles_of(xT):
    return [xT[:, k, :] for k in range(KT)]


class SquareSums:

    def __init__(self, sem, x_tiles, total, ring, wait_final):
        self.x_tiles, self.total, self.ring, self.wait_final = x_tiles, total, ring, wait_final
        self.squared, self.accumulated = sem("squared"), sem("accumulated")

    def square(self, act, n):
        for half in range(2):
            m = 2 * n + half
            self.wait_final(act, m)
            if m >= 2:
                act.wait_ge(self.accumulated, m - 1)
            act.activation(self.ring[:, half], self.x_tiles[n][:, half * HALF:(half + 1) * HALF], ACT.Square)\
                .then_inc(self.squared, 1)

    def accumulate(self, dve, n):
        for half in range(2):
            m = 2 * n + half
            total = self.total[:, half * HALF:(half + 1) * HALF]
            dve.wait_ge(self.squared, m + 1)
            if n == 0:
                dve.tensor_copy(total, self.ring[:, half]).then_inc(self.accumulated, 1)
            else:
                dve.wait_ge(self.accumulated, m - 1)
                dve.tensor_tensor(total, total, self.ring[:, half], ALU.add).then_inc(self.accumulated, 1)


class NormInput:

    def __init__(self, nc, ctx, name, sem, x_tiles, total, gain_dram, ones, ring, banks, hT_hi, hT_lo):
        self.x_tiles, self.rstd, self.ones, self.ring, self.banks = x_tiles, total, ones, ring, banks
        self.hT_hi, self.hT_lo, self.gain_dram = hT_hi, hT_lo, gain_dram
        self.gain = ctx.enter_context(nc.sbuf_tensor(f"{name}_norm_gain", [P, KT], F32))
        self.gain_in, self.summed, self.mean_done = sem("gain_in"), sem("summed"), sem("mean_done")
        self.root_done, self.rstd_done = sem("root_done"), sem("rstd_done")
        self.scaled, self.hi_done, self.even_lo, self.odd_lo = sem("scaled"), sem("hi_done"), sem("even_lo"), sem("odd_lo")

    @staticmethod
    def cols(s):
        return slice(s * HALF, (s + 1) * HALF)

    def load(self, sp):
        sp.dma_start(self.gain[:], self.gain_dram).then_inc(self.gain_in, 16)

    def sums(self, pe):
        for s in range(2):
            pe.matmul(self.banks[s][:], self.ones[:], self.rstd[:, self.cols(s)], start=True, stop=True)\
                .then_inc(self.summed, 1)

    def wait_tile(self, eng, s, k):
        i = s * KT + k
        if i % 2 == 0:
            eng.wait_ge(self.even_lo, i // 2 + 1)
        else:
            eng.wait_ge(self.odd_lo, i // 2 + 1)

    def wait_all(self, eng):
        eng.wait_ge(self.even_lo, KT)
        eng.wait_ge(self.odd_lo, KT)

    def roots(self, act):
        for s in range(2):
            act.wait_ge(self.mean_done, s + 1)
            act.activation(self.rstd[:, self.cols(s)], self.rstd[:, self.cols(s)], ACT.Sqrt).then_inc(self.root_done, 1)

    def high(self, act, s):
        for k in range(KT):
            i = s * KT + k
            act.wait_ge(self.scaled, i + 1)
            act.copy(self.hT_hi[:, k, self.cols(s)], self.ring[i % 3]).then_inc(self.hi_done, 1)

    def low(self, eng, s, k, done):
        i = s * KT + k
        eng.wait_ge(self.hi_done, i + 1)
        eng.tensor_tensor(self.hT_lo[:, k, self.cols(s)], self.ring[i % 3], self.hT_hi[:, k, self.cols(s)].bitcast(F32),
                          ALU.subtract).then_inc(done, 1)

    def odd_low(self, pool, s):
        for k in range(1, KT, 2):
            self.low(pool, s, k, self.odd_lo)

    def scale(self, dve):
        for s in range(2):
            dve.wait_ge(self.summed, s + 1)
            dve.tensor_scalar(self.rstd[:, self.cols(s)], self.banks[s][:], 1.0 / DM, EPS, ALU.mult, ALU.add)\
                .then_inc(self.mean_done, 1)
        dve.wait_ge(self.gain_in, 16)
        for s in range(2):
            dve.wait_ge(self.root_done, s + 1)
            dve.reciprocal(self.rstd[:, self.cols(s)], self.rstd[:, self.cols(s)]).then_inc(self.rstd_done, 1)
            dve.wait_ge(self.rstd_done, s + 1)
            for k in range(KT):
                i = s * KT + k
                if i >= 3:
                    self.wait_tile(dve, (i - 3) // KT, (i - 3) % KT)
                dve.scalar_tensor_tensor(self.ring[i % 3], self.x_tiles[k][:, self.cols(s)], self.gain[:, k:k + 1],
                                         self.rstd[:, self.cols(s)], ALU.mult, ALU.mult).then_inc(self.scaled, 1)
                if k % 2 == 1:
                    self.low(dve, s, k - 1, self.even_lo)



def constants_phase(nc, ones, ident, rel_bias, onehot, bias_dram, x_dram, x_tiles, total):
    with ExitStack() as ctx:
        sb = lambda n, s, d=F32: ctx.enter_context(nc.sbuf_tensor(n, s, d))
        sem = ctx.enter_context(phase_semaphores(nc, "const_"))
        rel = sb("rel", [REL_BUCKETS + 1, NG * HEADS])
        hot = sb("hot", [REL_BUCKETS + 1, NG, BIAS_LEN])
        vec = sb("vec", [HEADS, NG, BIAS_LEN])
        ps = ctx.enter_context(nc.psum_tensor("bias_ps", [HEADS, NG, HALF], F32))
        rel_in, hot_in, filled, zeroed = sem("rel_in"), sem("hot_in"), sem("filled"), sem("zeroed")
        bias_mm, bias_copied, bias_out = sem("bias_mm"), sem("bias_copied"), sem("bias_out")
        x_in = [sem(f"x_in{k}") for k in range(KT)]
        squares = SquareSums(sem, x_tiles, total, sb("squares", [P, 2, HALF]), lambda eng, m: eng.wait_ge(x_in[m // 2], 16))
        block = ctx.enter_context(nc.Block())

        @block.scalar
        def _(act):
            for n in range(KT):
                squares.square(act, n)

        @block.sync
        def _(sp):
            sp.dma_start(rel[0:REL_BUCKETS, :], rel_bias.rearrange("b g h -> b (g h)")).then_inc(rel_in, 16)
            sp.dma_start(hot[:], onehot.rearrange("g b x -> b g x")).then_inc(hot_in, 16)
            for k in range(KT):
                sp.dma_start(x_tiles[k], x_dram[k * P:(k + 1) * P, :]).then_inc(x_in[k], 16)
            sp.wait_ge(bias_copied, 1)
            sp.dma_start(bias_dram.rearrange("g h x -> h g x"), vec[:]).then_inc(bias_out, 16)
            sp.wait_ge(bias_out, 16)

        @block.gpsimd
        def _(pool):
            pool.memset(ones[:], 1.0)
            pool.memset(ident[:], 0.0).then_inc(zeroed, 1)
            pool.wait_ge(zeroed, 1)
            pool.affine_select(out=ident[:], in_=ident[:], compare_op=ALU.not_equal, fill=1.0,
                               base=0, pattern=[[-1, P]], channel_multiplier=1)

        @block.vector
        def _(dve):
            dve.memset(rel[REL_BUCKETS:REL_BUCKETS + 1, :], MASKED).then_inc(filled, 1)
            dve.wait_ge(bias_mm, NG)
            dve.tensor_copy(vec[:], ps[:, :, 0:BIAS_LEN]).then_inc(bias_copied, 1)
            for n in range(KT):
                squares.accumulate(dve, n)

        @block.tensor
        def _(pe):
            pe.wait_ge(rel_in, 16)
            pe.wait_ge(hot_in, 16)
            pe.wait_ge(filled, 1)
            for g in range(NG):
                pe.matmul(ps[:, g, 0:BIAS_LEN], rel[:, g * HEADS:(g + 1) * HEADS], hot[:, g, :],
                          start=True, stop=True).then_inc(bias_mm, 1)



LOOP_FIRST = 4
LOOP_ROUND = 6
LOOP_COUNT = 3
LAST_SUPER = SECTIONS + 2


def run_supersteps(eng, step):
    for st in range(LOOP_FIRST):
        for j in range(TT):
            step(0, st, j)
    with eng.Fori(0, LOOP_COUNT) as i:
        for st in range(LOOP_FIRST, LOOP_FIRST + LOOP_ROUND):
            for j in range(TT):
                step(i, st, j)
    for st in range(LOOP_FIRST + LOOP_ROUND * LOOP_COUNT, LAST_SUPER + 1):
        for j in range(TT):
            step(0, st, j)


class AttentionBuffers:

    def __init__(self, nc, ctx):
        sb = lambda n, s: ctx.enter_context(nc.sbuf_tensor(n, s, F32))
        self.vT = sb("vT", [P, 2, SEQ])
        self.o_g0 = sb("o_g0", [P, 2, SEQ])
        self.o_g2 = sb("o_g2", [P, 1, SEQ])
        self.w_bc = sb("w_bc", [P, 2, SEQ])
        self.prob = sb("prob", [P, 2, 2, 2 * P])
        self.x_tiles = [b[:, i, :] for b in (self.vT, self.o_g0, self.w_bc) for i in range(2)]
        self.x_tiles += [self.o_g2[:, 0, :], self.prob[:].rearrange("p a h k -> p (a h k)")]


def attention_phase(nc, ones, ident, buffers, total, norm_gain, hT_hi, hT_lo, wqkv, q_gain, k_gain, bias_dram, yT_dram):
    with ExitStack() as ctx:
        sb = lambda n, s, d=F32: ctx.enter_context(nc.sbuf_tensor(n, s, d))
        ps = lambda n, s: ctx.enter_context(nc.psum_tensor(n, s, F32))
        sem = ctx.enter_context(phase_semaphores(nc, "at_"))
        W3 = 3 * P
        raw = sb("raw", [P, 4, W3])
        w_hi = sb("w_hi", [P, 2, KT, W3], F32R)
        w_lo = sb("w_lo", [P, 2, KT, W3], F32R)
        gains = sb("gains", [P, 2, NG])
        qk_hi = sb("qk_hi", [P, 2, 2, SEQ], F32R)
        qk_lo = sb("qk_lo", [P, 2, 2, SEQ], F32R)
        v_hi = sb("v_hi", [P, 3, P], F32R)
        v_lo = sb("v_lo", [P, 3, P], F32R)
        sq = sb("sq", [P, 2 * P])
        qkn = sb("qkn", [P, 2, 2 * P])
        ss = sb("ss", [P, 4])
        var = sb("var", [P, 4])
        rs = sb("rs", [P, 4])
        held = sb("held", [P, 1])
        minus_half = sb("minus_half", [P, 4])
        bias = [sb(f"bias{g}", [P, 2, 2 * P if g < 2 else P]) for g in range(NG)]
        pT_hi = sb("pT_hi", [P, 2, 2 * P], F32R)
        pT_lo = sb("pT_lo", [P, 2, 2 * P], F32R)
        stat = sb("stat", [P, 2, 4 * TT])
        neg_max = sb("neg_max", [P, 2, 2 * TT])
        stat_rows = sb("stat_rows", [4 * TT, P])
        vT, w_bc, prob = buffers.vT, buffers.w_bc, buffers.prob
        o_raw = [buffers.o_g0, total[:].rearrange("p (o t) -> p o t", o=1), buffers.o_g2]
        ring = sb("ring", [P, HALF])
        compact = sb("compact", [64, NG, 2, 2, 16])
        top = sb("top", [64, 2, 16])
        diff = sb("diff", [64, NG, 2, 16])
        grown = sb("grown", [64, NG, 2, 16])
        part = sb("part", [64, NG, 2, 16])
        den = sb("den", [64, 2, 16])
        share = sb("share", [64, NG, 2, 16])

        ps_qk = [ps(f"ps_qk{i}", [P, HALF]) for i in range(2)]
        ps_v = ps("ps_v", [P, HALF])
        ps_t = ps("ps_t", [P, HALF])
        ps_s = [ps(f"ps_s{h}", [P, HALF]) for h in range(2)]
        ps_p = ps("ps_p", [P, HALF])
        ps_o = ps("ps_o", [P, HALF])

        stat_dram = nc.dram_tensor("stat_dram", [NG, 2, 2, SEQ], F32, kind="Internal").ap()
        share_dram = nc.dram_tensor("share_dram", [NG, 2, SEQ], F32, kind="Internal").ap()

        raw_in = [sem(f"raw_in{i}") for i in range(4)]
        gains_in = sem("gains_in")
        bias_in = [sem(f"bias_in{g}") for g in range(NG)]
        w_hi_done, w_lo_done = sem("w_hi_done"), sem("w_lo_done")
        qk_mm, v_mm, turned = sem("qk_mm"), sem("v_mm"), sem("turned")
        scored, p_turned, pv_done = sem("scored"), sem("p_turned"), sem("pv_done")
        squared, reduced, rs_done, qkn_done = sem("squared"), sem("reduced"), sem("rs_done"), sem("qkn_done")
        var_done = sem("var_done")
        turn_hi, turn_lo = sem("turn_hi"), sem("turn_lo")
        vT_done = sem("vT_done")
        maxed, neg_done, exp_done = sem("maxed"), sem("neg_done"), sem("exp_done")
        p_hi_done, p_lo_done, o_done = sem("p_hi_done"), sem("p_lo_done"), sem("o_done")
        rows_done, rows_out = sem("rows_done"), sem("rows_out")
        compact_in = [sem(f"compact_in{g}") for g in range(2)]
        merge, diff_done, grown_done, share_done = sem("merge"), sem("diff_done"), sem("grown_done"), sem("share_done")
        share_out, wbc_in = sem("share_out"), [sem(f"wbc_in{i}") for i in range(2)]
        y_step, y_out = sem("y_step"), sem("y_out")
        set_done, half_set = sem("set_done"), sem("half_set")
        norm = NormInput(nc, ctx, "attn", sem, buffers.x_tiles, total, norm_gain, ones,
                         [ring[:], qkn[:].rearrange("p a c -> p (a c)"), bias[1][:].rearrange("p h k -> p (h k)")], [ps_p, ps_o], hT_hi, hT_lo)
        block = ctx.enter_context(nc.Block())

        def has_unit(st, j, back):
            return TT <= TT * st + j - back < TT * (SECTIONS + 1)

        def unit(st, j, back):
            sec, u = divmod(TT * (st - 1) + j - back, TT)
            return sec, u

        def has_prev(g, u):
            return u > 0 if g == 0 else (u % 2 == 1 if g == 1 else False)

        @block.sync
        def _(sp):
            norm.load(sp)
            sp.dma_start(gains[0:HD, 0, :], q_gain).then_inc(gains_in, 16)
            sp.dma_start(gains[HD:P, 0, :], q_gain).then_inc(gains_in, 16)
            sp.dma_start(gains[0:HD, 1, :], k_gain).then_inc(gains_in, 16)
            sp.dma_start(gains[HD:P, 1, :], k_gain).then_inc(gains_in, 16)
            for n in range(TT + 4):
                if n >= 4:
                    sp.wait_ge(w_lo_done, n - 3)
                sp.dma_start(raw[:, n % 4], wqkv[n]).then_inc(raw_in[n % 4], 16)

            def step(i, st, j):
                N = st + 6 * i
                T = TT * N + j
                if TT * st + j + 12 < TT * SECTIONS:
                    sp.wait_ge(w_lo_done, T + 9)
                    sp.dma_start(raw[:, j % 4], wqkv[T + 12]).then_inc(raw_in[j % 4], 16)
                if j == 2 and st < SECTIONS:
                    g, pair = st % NG, st // NG + 2 * i
                    if st >= NG:
                        sp.wait_ge(neg_done, TT * N - 2 * TT)
                    if st == 1:
                        norm.wait_all(sp)
                    base = (g * HEADS + 2 * pair) * BIAS_LEN
                    if g < 2:
                        sp.dma_start(bias[g][:], bass.AP(bias_dram.tensor, base, [[1, P], [BIAS_LEN, 2], [1, 2 * P]]))\
                            .then_inc(bias_in[g], 16)
                    else:
                        sp.dma_start(bias[g][0:64], bass.AP(bias_dram.tensor, base, [[1, 64], [BIAS_LEN, 2], [1, P]]))\
                            .then_inc(bias_in[g], 16)
                        sp.dma_start(bias[g][64:P, :, 0:64],
                                     bass.AP(bias_dram.tensor, base + 64, [[1, 64], [BIAS_LEN, 2], [1, 64]]))\
                            .then_inc(bias_in[g], 16)
                if j == 2 and 2 <= st <= SECTIONS + 1 and (st - 2) % NG < 2:
                    g, pair = (st - 2) % NG, (st - 2) // NG + 2 * i
                    rows = 2 * pair + g + 1
                    sp.wait_ge(rows_done, rows)
                    sp.dma_start(stat_dram[g].rearrange("s h (u q) -> (s h u) q", q=P), stat_rows[:]).then_inc(rows_out, 16)
                    sp.wait_ge(rows_out, 16 * rows)
                    for s in range(2):
                        for h in range(2):
                            src = stat_dram[g, s, h]
                            if g == 0:
                                sp.dma_start(compact[:, g, s, h, :], src.rearrange("(p c) -> p c", c=16))\
                                    .then_inc(compact_in[g], 16)
                            else:
                                sp.dma_start(compact[:, g, s, h, :].rearrange("p (r c) -> p r c", r=4),
                                             src.rearrange("(r p c) -> p r c", r=4, c=4)).then_inc(compact_in[g], 16)
                if j == 5 and st >= 4 and (st - 4) % NG == 0:
                    pair = (st - 4) // NG + 2 * i
                    sp.wait_ge(share_done, pair + 1)
                    sp.dma_start(share_dram.rearrange("g h (p c) -> p (g h) c", c=16),
                                 share[:].rearrange("p g h c -> p (g h) c")).then_inc(share_out, 16)
                    sp.wait_ge(share_out, 16 * pair + 16)
                    for g in range(2):
                        for h in range(2):
                            sp.dma_start(w_bc[64 * h:64 * h + 64, g, :],
                                         share_dram[g, h:h + 1, :].to_broadcast([64, SEQ])).then_inc(wbc_in[g], 16)
                if j == 0 and st >= 5 and (st - 5) % NG == 0:
                    pair = (st - 5) // NG + 2 * i
                    sp.wait_ge(y_step, 5 * pair + 1)
                    for h in range(2):
                        sp.dma_start(w_bc[64 * h:64 * h + 64, 0, :],
                                     share_dram[2, h:h + 1, :].to_broadcast([64, SEQ])).then_inc(wbc_in[0], 16)
                if j == 5 and st >= 5 and (st - 5) % NG == 0:
                    pair, par = (st - 5) // NG + 2 * i, ((st - 5) // NG) % 2
                    sp.wait_ge(y_step, 5 * pair + 5)
                    sp.dma_start(yT_dram[pair], o_raw[0][:, par, :]).then_inc(y_out, 16)

            run_supersteps(sp, step)
            sp.wait_ge(y_out, 16 * PAIRS)

        @block.tensor
        def _(pe):
            def step(i, st, j):
                N = st + 6 * i
                T = TT * N + j
                U = T - TT
                par = st % 2
                if st < SECTIONS:
                    if st >= 1 or j >= 2:
                        pe.wait_ge(qkn_done, T - 1)
                    for k in range(KT):
                        if st == 0 and j % 4 == 0:
                            norm.wait_tile(pe, j // 4, k)
                        if j == 0:
                            pe.wait_ge(w_hi_done, TT * N + k + 1)
                            pe.wait_ge(w_lo_done, TT * N + k + 1)
                        mm = split_matmul(pe, ps_qk[j % 2][:, 0:2 * P],
                                          hT_hi[:, k, j * P:(j + 1) * P], hT_lo[:, k, j * P:(j + 1) * P],
                                          w_hi[:, par, k, 0:2 * P], w_lo[:, par, k, 0:2 * P], k == 0, k == KT - 1)
                    mm.then_inc(qk_mm, 1)
                if (st >= 1 or j >= 1) and st <= SECTIONS:
                    if TT * st + j >= 2:
                        pe.wait_ge(turn_hi, T - 1)
                        pe.wait_ge(turn_lo, T - 1)
                    if TT * st + j - 1 < TT * SECTIONS:
                        pe.wait_ge(qkn_done, T)
                        for a in range(2):
                            mm = pe.transpose(ps_t[:, a * P:(a + 1) * P], qkn[:, (j - 1) % 2, a * P:(a + 1) * P], ident[:])
                    if st >= 1:
                        if j == 0:
                            pe.wait_ge(vT_done, 2 * N)
                        mm = pe.transpose(ps_t[:, 2 * P:3 * P], vT[:, (st - 1) % 2, j * P:(j + 1) * P], ident[:])
                    if j == 1 and st >= 2 and (st - 2) % NG < 2:
                        pe.wait_ge(exp_done, U - 1)
                        pe.wait_ge(neg_done, U - 1)
                        mm = pe.transpose(ps_t[0:4 * TT, 3 * P:4 * P], stat[:, (st - 2) % 2, :], ident[:])
                    mm.then_inc(turned, 1)
                if has_unit(st, j, 1):
                    sec, u = unit(st, j, 1)
                    g = sec % NG
                    pe.wait_ge(exp_done, U)
                    if has_unit(st, j, 2):
                        pe.wait_ge(p_hi_done, U - 1)
                        pe.wait_ge(p_lo_done, U - 1)
                    for h in range(2):
                        for b in range(0 if has_prev(g, u) else 1, 2):
                            c = (2 * b + h) * P
                            mm = pe.transpose(ps_p[:, c:c + P], prob[:, u % 2, h, b * P:(b + 1) * P], ident[:])
                    mm.then_inc(p_turned, 1)
                if st < SECTIONS:
                    half = j // 4
                    if j == 0 and st >= 1:
                        pe.wait_ge(vT_done, 2 * N)
                    if j == 4:
                        pe.wait_ge(vT_done, 2 * N + 1)
                    for k in range(2 * (j % 4), 2 * (j % 4) + 2):
                        mm = split_matmul(pe, ps_v[:], w_hi[:, par, k, 2 * P:3 * P], w_lo[:, par, k, 2 * P:3 * P],
                                          hT_hi[:, k, half * HALF:(half + 1) * HALF],
                                          hT_lo[:, k, half * HALF:(half + 1) * HALF], k == 0, k == KT - 1)
                    if j % 4 == 3:
                        mm.then_inc(v_mm, 1)
                if has_unit(st, j, 0):
                    sec, u = unit(st, j, 0)
                    g, sp_ = sec % NG, sec % 2
                    if j == 0:
                        pe.wait_ge(turn_hi, T)
                        pe.wait_ge(turn_lo, T)
                    if has_unit(st, j, 1):
                        pe.wait_ge(exp_done, U)
                    k0 = (u - 1) * P if has_prev(g, u) else u * P
                    c0 = 0 if has_prev(g, u) else P
                    for h in range(2):
                        rows = slice(HD * h, HD * h + HD)
                        mm = split_matmul(pe, ps_s[h][:, c0:2 * P],
                                          qk_hi[rows, sp_, 0, u * P:(u + 1) * P], qk_lo[rows, sp_, 0, u * P:(u + 1) * P],
                                          qk_hi[rows, sp_, 1, k0:(u + 1) * P], qk_lo[rows, sp_, 1, k0:(u + 1) * P],
                                          True, True)
                    mm.then_inc(scored, 1)
                if has_unit(st, j, 1):
                    sec, u = unit(st, j, 1)
                    g = sec % NG
                    whole = TT * sec + u
                    pe.wait_ge(p_hi_done, U)
                    pe.wait_ge(p_lo_done, U)
                    if has_unit(st, j, 2):
                        pe.wait_ge(o_done, U - 1)
                    first = 0 if has_prev(g, u) else 1
                    for b in range(first, 2):
                        slot = (whole - 1 + b) % 3
                        mm = split_matmul(pe, ps_o[:, 0:2 * P], v_hi[:, slot, :], v_lo[:, slot, :],
                                          pT_hi[:, b, :], pT_lo[:, b, :], b == first, b == 1)
                    mm.then_inc(pv_done, 1)

            norm.sums(pe)
            run_supersteps(pe, step)

        @block.scalar
        def _(act):
            def hi_part(n, slot, par, k):
                act.copy(w_hi[:, par, k, :], raw[:, slot, :]).then_inc(w_hi_done, 1)

            act.wait_ge(set_done, 2)
            norm.roots(act)
            for k in range(KT):
                act.wait_ge(raw_in[k % 4], 16 * (k // 4 + 1))
                hi_part(k, k % 4, 0, k)
                if k % 4 == 3:
                    norm.high(act, k // 4)
            norm.wait_all(act)

            def step(i, st, j):
                N = st + 6 * i
                T = TT * N + j
                U = T - TT
                par = st % 2
                if j == 0 and 1 <= st <= SECTIONS:
                    act.wait_ge(v_mm, 2 * N)
                    g, vp = (st - 1) % NG, (st - 1) % 2
                    act.copy(perm_dest(vT[:, vp, :], g, HALF, HALF), perm_view(ps_v[:], g, HALF)).then_inc(vT_done, 1)
                if j == 4 and st < SECTIONS:
                    act.wait_ge(v_mm, 2 * N + 1)
                    g = st % NG
                    act.copy(perm_dest(vT[:, par, :], g, 0, HALF), perm_view(ps_v[:], g, HALF)).then_inc(vT_done, 1)
                if has_unit(st, j, 1):
                    sec, u = unit(st, j, 1)
                    g, sp_ = sec % NG, sec % 2
                    act.wait_ge(neg_done, U)
                    if has_unit(st, j, 3):
                        act.wait_ge(p_turned, U - 2)
                    c0 = 0 if has_prev(g, u) else P
                    for h in range(2):
                        a = act.activation(prob[:, u % 2, h, c0:2 * P], ps_s[h][:, c0:2 * P], ACT.Exp,
                                           bias=neg_max[:, sp_, h * TT + u:h * TT + u + 1],
                                           accum_out=stat[:, sp_, (2 + h) * TT + u:(2 + h) * TT + u + 1])
                    a.then_inc(exp_done, 1)
                if has_unit(st, j, 2):
                    sec, u = unit(st, j, 2)
                    g = sec % NG
                    act.wait_ge(pv_done, U - 1)
                    if u == 0:
                        pair_st = sec // NG
                        if g == 0 and pair_st >= 2:
                            act.wait_ge(y_out, 16 * (pair_st + 2 * i) - 16)
                        if g >= 1 and pair_st >= 1:
                            act.wait_ge(y_step, 5 * (pair_st + 2 * i) - 5 + 2 * g)
                    ob = o_raw[g][:, (sec // NG) % 2 if g == 0 else 0, :]
                    act.copy(ob[0:HD, u * P:(u + 1) * P], ps_o[0:HD, 0:P])
                    act.copy(ob[HD:P, u * P:(u + 1) * P], ps_o[HD:P, P:2 * P]).then_inc(o_done, 1)
                if j == 3 and st >= 4 and (st - 4) % NG == 0:
                    act.wait_ge(diff_done, (st - 4) // NG + 2 * i + 1)
                    act.activation(grown[:], diff[:], ACT.Exp).then_inc(grown_done, 1)
                if st + 1 < SECTIONS:
                    if j == 0 and st >= 1:
                        act.wait_ge(qk_mm, TT * N)
                        act.wait_ge(v_mm, 2 * N)
                    act.wait_ge(raw_in[j % 4], 32 * N + 16 * (3 + j // 4))
                    hi_part(T, j % 4, (st + 1) % 2, j)
                if st < SECTIONS:
                    act.wait_ge(qk_mm, T + 1)
                    if TT * st + j >= 1:
                        act.wait_ge(reduced, T)
                    act.activation(sq[:], ps_qk[j % 2][:, 0:2 * P], ACT.Square).then_inc(squared, 1)
                def turned_probabilities():
                    if has_unit(st, j, 1):
                        sec, u = unit(st, j, 1)
                        b0 = 0 if has_prev(sec % NG, u) else 1
                        act.wait_ge(p_turned, U)
                        act.copy(pT_hi[:, b0:2, :],
                                 ps_p[:].rearrange("p (b c) -> p b c", b=2)[:, b0:2, :]).then_inc(p_hi_done, 1)

                def turned_tiles():
                    if (st >= 1 or j >= 1) and st <= SECTIONS:
                        act.wait_ge(turned, T)
                        if TT * st + j - 1 < TT * SECTIONS:
                            sec, t = divmod(TT * st + j - 1, TT)
                            g = sec % NG
                            for a in range(2):
                                ins = act.activation(perm_dest(qk_hi[:, sec % 2, a, :], g, t * P, P),
                                                     perm_view(ps_t[:, a * P:(a + 1) * P], g, P), ACT.Copy,
                                                     scale=gains[:, a, g:g + 1])
                        if st >= 1:
                            ins = act.copy(v_hi[:, (TT * (st - 1) + j) % 3, :], ps_t[:, 2 * P:3 * P])
                        ins.then_inc(turn_hi, 1)

                if j == 0:
                    turned_tiles()
                    turned_probabilities()
                else:
                    turned_probabilities()
                    turned_tiles()

            run_supersteps(act, step)

        @block.vector
        def _(dve):
            dve.memset(bias[2][64:P, :, 64:P], MASKED).then_inc(set_done, 1)
            dve.wait_ge(gains_in, 64)
            dve.tensor_scalar(gains[:, 0, :], gains[:, 0, :], HD ** -0.5, None, ALU.mult).then_inc(set_done, 1)
            def step(i, st, j):
                N = st + 6 * i
                T = TT * N + j
                U = T - TT
                if has_unit(st, j, 1):
                    sec, u = unit(st, j, 1)
                    g, sp_ = sec % NG, sec % 2
                    n = 2 * P if has_prev(g, u) else P
                    if u == 0:
                        per = 16 if g < 2 else 32
                        dve.wait_ge(bias_in[g], per * (sec // NG + 2 * i) + per)
                    dve.wait_ge(scored, U)
                    dve.memset(held[:], 0.0)
                    for h in range(2):
                        width = 2 * P if g < 2 else P
                        rev = bass.AP(bias[g][:].tensor, h * width + n - 1, [[2 * width, P], [-1, n]])
                        s = ps_s[h][:, 2 * P - n:2 * P]
                        dve.tensor_tensor_reduce(s, s, rev, 1.0, -3.0e38, ALU.add, ALU.max,
                                                 stat[:, sp_, h * TT + u:h * TT + u + 1]).then_inc(maxed, 1)
                    dve.wait_ge(maxed, 2 * U)
                    dve.tensor_scalar(neg_max[:, sp_, u:2 * TT:TT], stat[:, sp_, u:2 * TT:TT], -1.0, None,
                                      ALU.mult).then_inc(neg_done, 1)
                if st < SECTIONS:
                    dve.wait_ge(squared, T + 1)
                    if TT * st + j >= 1:
                        dve.wait_ge(var_done, T)
                    dve.tensor_reduce(ss[:], sq[:].rearrange("p (h e) -> p h e", e=HD), AX.X, ALU.add)\
                        .then_inc(reduced, 1)
                    dve.wait_ge(reduced, T + 1)
                    if TT * st + j >= 1:
                        dve.wait_ge(rs_done, T)
                    dve.tensor_scalar(var[:], ss[:], 1.0 / HD, EPS, ALU.mult, ALU.add).then_inc(var_done, 1)
                def turned_probabilities():
                    if has_unit(st, j, 1):
                        sec, u = unit(st, j, 1)
                        b0 = 0 if has_prev(sec % NG, u) else 1
                        dve.wait_ge(p_hi_done, U)
                        dve.tensor_tensor(pT_lo[:, b0:2, :], ps_p[:].rearrange("p (b c) -> p b c", b=2)[:, b0:2, :],
                                          pT_hi[:, b0:2, :].bitcast(F32), ALU.subtract).then_inc(p_lo_done, 1)

                def turned_tiles():
                    if (st >= 1 or j >= 1) and st <= SECTIONS:
                        dve.wait_ge(turn_hi, T)
                        if j == 1 and st >= 2 and (st - 2) % NG < 2:
                            if st >= 3:
                                dve.wait_ge(rows_out, 16 * (2 * ((st - 2) // NG + 2 * i) + (st - 2) % NG))
                            dve.tensor_copy(stat_rows[:], ps_t[0:4 * TT, 3 * P:4 * P]).then_inc(rows_done, 1)
                        if TT * st + j - 1 < TT * SECTIONS:
                            sec, t = divmod(TT * st + j - 1, TT)
                            g = sec % NG
                            for a in range(2):
                                ins = dve.scalar_tensor_tensor(
                                    perm_dest(qk_lo[:, sec % 2, a, :], g, t * P, P),
                                    perm_view(ps_t[:, a * P:(a + 1) * P], g, P), gains[:, a, g:g + 1],
                                    perm_dest(qk_hi[:, sec % 2, a, :].bitcast(F32), g, t * P, P), ALU.mult, ALU.subtract)
                        if st >= 1:
                            slot = (TT * (st - 1) + j) % 3
                            ins = dve.tensor_tensor(v_lo[:, slot, :], ps_t[:, 2 * P:3 * P], v_hi[:, slot, :].bitcast(F32),
                                                    ALU.subtract)
                        ins.then_inc(turn_lo, 1)

                if j == 0:
                    turned_tiles()
                    turned_probabilities()
                else:
                    turned_probabilities()
                    turned_tiles()
                if st < SECTIONS:
                    dve.wait_ge(rs_done, T + 1)
                    if TT * st + j >= 2:
                        dve.wait_ge(turned, T - 1)
                    dve.tensor_tensor(qkn[:, j % 2, :].rearrange("p (h e) -> p h e", e=HD),
                                      ps_qk[j % 2][:, 0:2 * P].rearrange("p (h e) -> p h e", e=HD),
                                      rs[:].rearrange("p (h o) -> p h o", o=1).to_broadcast([P, 4, HD]), ALU.mult)\
                        .then_inc(qkn_done, 1)
                merge_step(i, st, j)

            def merge_step(i, st, j):
                if st >= 4 and (st - 4) % NG == 0:
                    pair = (st - 4) // NG + 2 * i
                    base = 10 * pair
                    if j == 1:
                        dve.wait_ge(exp_done, TT * (st + 6 * i) - TT)
                        for half in range(2):
                            dve.tensor_copy(compact[:, 2, :, :, half:16:2],
                                            stat[64 * half:64 * half + 64, (st - 2) % 2, :]
                                            .rearrange("p (s h u) -> p s h u", s=2, h=2)).then_inc(merge, 1)
                    m = [compact[:, 0, 0], compact[:, 1, 0].rearrange("p h (r c) -> p h c r", r=4), compact[:, 2, 0]]
                    d = [compact[:, 0, 1], compact[:, 1, 1].rearrange("p h (r c) -> p h c r", r=4), compact[:, 2, 1]]
                    nat = lambda ap, g: ap.rearrange("p h (c r) -> p h c r", r=4) if g == 1 else ap
                    if j == 2:
                        dve.wait_ge(compact_in[0], 64 * pair + 64)
                        dve.wait_ge(compact_in[1], 64 * pair + 64)
                        dve.wait_ge(merge, base + 2)
                        dve.tensor_tensor(top[:], m[0], m[2], ALU.max).then_inc(merge, 1)
                        dve.wait_ge(merge, base + 3)
                        dve.tensor_tensor(nat(top[:], 1), nat(top[:], 1), m[1], ALU.max).then_inc(merge, 1)
                        dve.wait_ge(merge, base + 4)
                        for g in range(NG):
                            ins = dve.tensor_tensor(nat(diff[:, g], g), m[g], nat(top[:], g), ALU.subtract)
                        ins.then_inc(diff_done, 1)
                    if j == 4:
                        dve.wait_ge(grown_done, pair + 1)
                        for g in range(NG):
                            dve.tensor_tensor(nat(part[:, g], g), nat(grown[:, g], g), d[g], ALU.mult).then_inc(merge, 1)
                        dve.wait_ge(merge, base + 7)
                        dve.tensor_tensor(den[:], part[:, 0], part[:, 1], ALU.add).then_inc(merge, 1)
                        dve.wait_ge(merge, base + 8)
                        dve.tensor_tensor(den[:], den[:], part[:, 2], ALU.add).then_inc(merge, 1)
                        dve.wait_ge(merge, base + 9)
                        dve.reciprocal(den[:], den[:]).then_inc(merge, 1)
                        dve.wait_ge(merge, base + 10)
                        for g in range(NG):
                            ins = dve.tensor_tensor(share[:, g], grown[:, g], den[:], ALU.mult)
                        ins.then_inc(share_done, 1)
                    if j == 7:
                        o0 = o_raw[0][:, ((st - 4) // NG) % 2, :]
                        dve.wait_ge(wbc_in[0], 64 * pair + 32)
                        dve.wait_ge(o_done, TT * (st + 6 * i) - TT)
                        dve.tensor_tensor(o0, o0, w_bc[:, 0, :], ALU.mult).then_inc(y_step, 1)
                if st >= 5 and (st - 5) % NG == 0:
                    pair = (st - 5) // NG + 2 * i
                    o0 = o_raw[0][:, ((st - 5) // NG) % 2, :]
                    if j == 1:
                        dve.wait_ge(wbc_in[1], 32 * pair + 32)
                        w = split_tokens(w_bc[:, 1, :], 1)
                        dve.tensor_tensor(w, w, natural_view(o_raw[1][:, 0, :], 1), ALU.mult).then_inc(y_step, 1)
                    if j == 2:
                        dve.wait_ge(y_step, 5 * pair + 2)
                        dve.tensor_tensor(o0, o0, w_bc[:, 1, :], ALU.add).then_inc(y_step, 1)
                    if j == 3:
                        dve.wait_ge(wbc_in[0], 64 * pair + 64)
                        w = split_tokens(w_bc[:, 0, :], 2)
                        dve.tensor_tensor(w, w, natural_view(o_raw[2][:, 0, :], 2), ALU.mult).then_inc(y_step, 1)
                    if j == 4:
                        dve.wait_ge(y_step, 5 * pair + 4)
                        dve.tensor_tensor(o0, o0, w_bc[:, 0, :], ALU.add).then_inc(y_step, 1)

            norm.scale(dve)
            norm.wait_all(dve)
            dve.wait_ge(set_done, 2)
            run_supersteps(dve, step)

        @block.gpsimd
        def _(pool):
            def lo_part(slot, par, k):
                pool.tensor_tensor(w_lo[:, par, k, :], raw[:, slot, :], w_hi[:, par, k, :].bitcast(F32),
                                   ALU.subtract).then_inc(w_lo_done, 1)

            pool.memset(minus_half[:], -0.5).then_inc(half_set, 1)
            for k in range(KT):
                pool.wait_ge(w_hi_done, k + 1)
                lo_part(k % 4, 0, k)
                if k % 4 == 3:
                    norm.odd_low(pool, k // 4)
            pool.wait_ge(half_set, 1)

            def step(i, st, j):
                N = st + 6 * i
                T = TT * N + j
                if st + 1 < SECTIONS:
                    pool.wait_ge(w_hi_done, T + TT + 1)
                    lo_part(j % 4, (st + 1) % 2, j)
                if st < SECTIONS:
                    pool.wait_ge(var_done, T + 1)
                    if TT * st + j >= 1:
                        pool.wait_ge(qkn_done, T)
                    pool.tensor_tensor(rs[:], var[:], minus_half[:], ALU.pow).then_inc(rs_done, 1)

            run_supersteps(pool, step)



RAW_SLOTS = 4


def project_phase(nc, name, xT, total, w_pieces, yT, yT_dram, x_dram):
    with ExitStack() as ctx:
        sb = lambda n, s, d=F32: ctx.enter_context(nc.sbuf_tensor(f"{name}_{n}", s, d))
        sem = ctx.enter_context(phase_semaphores(nc, f"{name}_"))
        raw = sb("raw", [P, RAW_SLOTS, DM])
        w_hi = sb("w_hi", [P, 2, KT, P], F32R)
        w_lo = sb("w_lo", [P, 2, KT, P], F32R)
        yT_hi = sb("yT_hi", [P, KT, SEQ], F32R)
        yT_lo = sb("yT_lo", [P, KT, SEQ], F32R)
        y_raw = sb("y_raw", [P, 2, SEQ]) if yT is None else None
        ps = [ctx.enter_context(nc.psum_tensor(f"{name}_ps{i}", [P, HALF], F32)) for i in range(8)]
        raw_in = [sem(f"raw_in{i}") for i in range(RAW_SLOTS)]
        y_in = [sem(f"y_in{i}") for i in range(2)]
        x_in = sem("x_in")
        w_hi_done, w_lo_done, y_hi_done, y_lo_done = sem("w_hi_done"), sem("w_lo_done"), sem("y_hi_done"), sem("y_lo_done")
        product, x_added = sem("product"), sem("x_added")
        load = yT is None
        squares = SquareSums(sem, tiles_of(xT), total, sb("squares", [P, 2, HALF]), lambda eng, m: eng.wait_ge(x_added, m + 1))

        def y_tile(k):
            return y_raw[:, k % 2, :] if load else yT[:, k, :]

        block = ctx.enter_context(nc.Block())

        @block.sync
        def _(sp):
            for k in range(KT):
                if k < RAW_SLOTS:
                    sp.dma_start(raw[:, k, :], w_pieces[k]).then_inc(raw_in[k], 16)
                if load:
                    if k >= 2:
                        sp.wait_ge(y_lo_done, k - 1)
                    sp.dma_start(y_raw[:, k % 2, :], yT_dram[k]).then_inc(y_in[k % 2], 16)
            if load:
                sp.dma_start(xT[:], x_dram.rearrange("(k p) t -> p k t", p=P)).then_inc(x_in, 16)
            for n in range(RAW_SLOTS, KT):
                sp.wait_ge(w_lo_done, n - RAW_SLOTS + 1)
                sp.dma_start(raw[:, n % RAW_SLOTS, :], w_pieces[n]).then_inc(raw_in[n % RAW_SLOTS], 16)

        @block.scalar
        def _(act):
            for n in range(KT):
                if load:
                    act.wait_ge(y_in[n % 2], 16 * (n // 2 + 1))
                act.copy(yT_hi[:, n, :], y_tile(n)).then_inc(y_hi_done, 1)
                if n >= 1:
                    continue
                act.wait_ge(raw_in[0], 16)
                act.copy(w_hi[:, 0].rearrange("p k c -> p (k c)"), raw[:, 0, :]).then_inc(w_hi_done, 1)
            for n in range(1, KT):
                act.wait_ge(raw_in[n % RAW_SLOTS], 16 * (n // RAW_SLOTS + 1))
                if n >= 2:
                    act.wait_ge(product, 2 * (n - 1))
                act.copy(w_hi[:, n % 2].rearrange("p k c -> p (k c)"), raw[:, n % RAW_SLOTS, :]).then_inc(w_hi_done, 1)
                if n >= 2:
                    squares.square(act, n - 2)
            squares.square(act, KT - 2)
            squares.square(act, KT - 1)

        @block.gpsimd
        def _(pool):
            for n in range(KT):
                pool.wait_ge(w_hi_done, n + 1)
                pool.tensor_tensor(w_lo[:, n % 2].rearrange("p k c -> p (k c)"), raw[:, n % RAW_SLOTS, :],
                                   w_hi[:, n % 2].rearrange("p k c -> p (k c)").bitcast(F32),
                                   ALU.subtract).then_inc(w_lo_done, 1)

        @block.tensor
        def _(pe):
            for n in range(KT):
                pe.wait_ge(w_lo_done, n + 1)
                for half in range(2):
                    if n >= 4:
                        pe.wait_ge(x_added, 2 * (n - 4) + half + 1)
                    cols = slice(half * HALF, (half + 1) * HALF)
                    for k in range(KT):
                        if n == 0:
                            pe.wait_ge(y_lo_done, k + 1)
                        mm = split_matmul(pe, ps[(2 * n + half) % 8][:], w_hi[:, n % 2, k, :], w_lo[:, n % 2, k, :],
                                          yT_hi[:, k, cols], yT_lo[:, k, cols], k == 0, k == KT - 1)
                    mm.then_inc(product, 1)

        @block.vector
        def _(dve):
            for k in range(KT):
                dve.wait_ge(y_hi_done, k + 1)
                dve.tensor_tensor(yT_lo[:, k, :], y_tile(k), yT_hi[:, k, :].bitcast(F32), ALU.subtract).then_inc(y_lo_done, 1)
            if load:
                dve.wait_ge(x_in, 16)
            for n in range(KT):
                for half in range(2):
                    cols = slice(half * HALF, (half + 1) * HALF)
                    dve.wait_ge(product, 2 * n + half + 1)
                    dve.tensor_tensor(xT[:, n, cols], xT[:, n, cols], ps[(2 * n + half) % 8][:],
                                      ALU.add).then_inc(x_added, 1)
                if n >= 2:
                    squares.accumulate(dve, n - 2)
            squares.accumulate(dve, KT - 2)
            squares.accumulate(dve, KT - 1)


def mlp_phase(nc, name, xT, total, gain, ones, w1_pieces, w2_pieces, hT_hi, hT_lo, out_dram):
    with ExitStack() as ctx:
        sb = lambda n, s, d=F32: ctx.enter_context(nc.sbuf_tensor(f"{name}_{n}", s, d))
        sem = ctx.enter_context(phase_semaphores(nc, f"{name}_"))
        PIECES = 2 * KT
        raw = sb("raw", [P, RAW_SLOTS, DM])
        w_hi = sb("w_hi", [P, 2, KT, P], F32R)
        w_lo = sb("w_lo", [P, 2, KT, P], F32R)
        hid_hi = sb("hid_hi", [P, KT, SEQ], F32R)
        hid_lo = sb("hid_lo", [P, KT, SEQ], F32R)
        positive = sb("positive", [P, 2, HALF])
        squared = sb("squared", [P, HALF])
        ps = [ctx.enter_context(nc.psum_tensor(f"{name}_ps{i}", [P, HALF], F32)) for i in range(8)]
        raw_in = [sem(f"raw_in{i}") for i in range(RAW_SLOTS)]
        w_hi_done, w_lo_done, product = sem("w_hi_done"), sem("w_lo_done"), sem("product")
        relu_done, square_done, hid_hi_done, hid_lo_done = sem("relu_done"), sem("square_done"), sem("hid_hi_done"), sem("hid_lo_done")
        x_added, stored = sem("x_added"), sem("stored")
        norm = NormInput(nc, ctx, name, sem, tiles_of(xT), total, gain, ones, [positive[:, 0], positive[:, 1], squared[:]],
                         ps[0:2], hT_hi, hT_lo)
        squares = None
        if out_dram is None:
            squares = SquareSums(sem, tiles_of(xT), total, positive, lambda eng, m: eng.wait_ge(x_added, 2 * KT * (FCH - 1) + m + 1))
        block = ctx.enter_context(nc.Block())

        def run_chunks(eng, chunk):
            chunk(0, True, False)
            with eng.Fori(1, FCH - 1) as c:
                chunk(c, False, False)
            chunk(FCH - 1, False, True)

        @block.sync
        def _(sp):
            def piece(c, q):
                return w1_pieces[c, q] if q < KT else w2_pieces[c, q - KT]

            def load(c, q):
                sp.dma_start(raw[:, q % RAW_SLOTS, :], piece(c, q)).then_inc(raw_in[q % RAW_SLOTS], 16)

            def chunk(c, first, last):
                for q in range(PIECES):
                    if not first or q >= RAW_SLOTS:
                        sp.wait_ge(w_lo_done, PIECES * c + q - RAW_SLOTS + 1)
                    load(c, q)

            norm.load(sp)
            run_chunks(sp, chunk)
            if out_dram is not None:
                for d in range(KT):
                    sp.wait_ge(x_added, 2 * KT * (FCH - 1) + 2 * d + 2)
                    sp.dma_start(out_dram[d], xT[:, d, :]).then_inc(stored, 16)
                sp.wait_ge(stored, 16 * KT)

        @block.scalar
        def _(act):
            def hi_part(c, q, first):
                n = PIECES * c + q
                act.wait_ge(raw_in[q % RAW_SLOTS], 16 * (PIECES // RAW_SLOTS) * c + 16 * (q // RAW_SLOTS + 1))
                if not first or q >= 2:
                    act.wait_ge(product, 2 * n - 2)
                act.copy(w_hi[:, q % 2].rearrange("p k c -> p (k c)"), raw[:, q % RAW_SLOTS, :]).then_inc(w_hi_done, 1)

            def chunk(c, first, last):
                if not first:
                    hi_part(c, 0, False)
                for q in range(PIECES):
                    if (q >= 1 or not first) and q + 1 < PIECES:
                        hi_part(c, q + 1, first)
                    if last and squares and q == KT:
                        act.wait_ge(square_done, 2 * KT * FCH)
                        act.wait_ge(hid_hi_done, 2 * KT * FCH)
                    if last and squares and q > KT:
                        squares.square(act, q - KT - 1)
                    if q < KT:
                        for half in range(2):
                            m = 2 * KT * c + 2 * q + half
                            act.wait_ge(product, 2 * PIECES * c + 2 * q + half + 1)
                            if not first or q >= 1:
                                act.wait_ge(square_done, m - 1)
                            act.activation(positive[:, half, :], ps[(2 * q + half) % 8][:], ACT.Relu).then_inc(relu_done, 1)
                            act.wait_ge(relu_done, m + 1)
                            act.activation(hid_hi[:, q, half * HALF:(half + 1) * HALF], positive[:, half, :],
                                           ACT.Square).then_inc(hid_hi_done, 1)

            norm.roots(act)
            hi_part(0, 0, True)
            norm.high(act, 0)
            hi_part(0, 1, True)
            norm.high(act, 1)
            norm.wait_all(act)
            run_chunks(act, chunk)
            if squares:
                squares.square(act, KT - 1)

        @block.gpsimd
        def _(pool):
            def lo_part(c, q):
                pool.wait_ge(w_hi_done, PIECES * c + q + 1)
                pool.tensor_tensor(w_lo[:, q % 2].rearrange("p k c -> p (k c)"), raw[:, q % RAW_SLOTS, :],
                                   w_hi[:, q % 2].rearrange("p k c -> p (k c)").bitcast(F32),
                                   ALU.subtract).then_inc(w_lo_done, 1)

            def chunk(c, first, last):
                for q in range(2 if first else 0, PIECES):
                    lo_part(c, q)

            for s in range(2):
                lo_part(0, s)
                norm.odd_low(pool, s)
            run_chunks(pool, chunk)

        @block.tensor
        def _(pe):
            def chunk(c, first, last):
                for q in range(PIECES):
                    pe.wait_ge(w_lo_done, PIECES * c + q + 1)
                    src_hi, src_lo = (hT_hi, hT_lo) if q < KT else (hid_hi, hid_lo)
                    for half in range(2):
                        cols = slice(half * HALF, (half + 1) * HALF)
                        if q >= 4 and q - 4 < KT:
                            pe.wait_ge(relu_done, 2 * KT * c + 2 * (q - 4) + half + 1)
                        elif q >= 4:
                            pe.wait_ge(x_added, 2 * KT * c + 2 * (q - 4 - KT) + half + 1)
                        elif not first:
                            pe.wait_ge(x_added, 2 * KT * c + 2 * (q - 4) + half + 1)
                        for k in range(KT):
                            if q == 0 and first:
                                norm.wait_tile(pe, half, k)
                            if q == KT:
                                pe.wait_ge(hid_lo_done, 2 * KT * c + 2 * k + half + 1)
                            mm = split_matmul(pe, ps[(2 * q + half) % 8][:], w_hi[:, q % 2, k, :], w_lo[:, q % 2, k, :],
                                              src_hi[:, k, cols], src_lo[:, k, cols], k == 0, k == KT - 1)
                        mm.then_inc(product, 1)

            norm.sums(pe)
            run_chunks(pe, chunk)

        @block.vector
        def _(dve):
            def chunk(c, first, last):
                for q in range(PIECES):
                    if last and squares and q > KT + 1:
                        squares.accumulate(dve, q - KT - 2)
                    for half in range(2):
                        cols = slice(half * HALF, (half + 1) * HALF)
                        m = 2 * KT * c + 2 * (q % KT) + half
                        if q < KT:
                            dve.wait_ge(relu_done, m + 1)
                            if not first or q > 0 or half > 0:
                                dve.wait_ge(hid_lo_done, m)
                            dve.tensor_tensor(squared[:], positive[:, half, :], positive[:, half, :],
                                              ALU.mult).then_inc(square_done, 1)
                            dve.wait_ge(square_done, m + 1)
                            dve.wait_ge(hid_hi_done, m + 1)
                            dve.tensor_tensor(hid_lo[:, q, cols], squared[:], hid_hi[:, q, cols].bitcast(F32),
                                              ALU.subtract).then_inc(hid_lo_done, 1)
                        else:
                            dve.wait_ge(product, 2 * PIECES * c + 2 * q + half + 1)
                            if not first:
                                dve.wait_ge(x_added, m - 2 * KT + 1)
                            dve.tensor_tensor(xT[:, q - KT, cols], xT[:, q - KT, cols], ps[(2 * q + half) % 8][:],
                                              ALU.add).then_inc(x_added, 1)

            norm.scale(dve)
            norm.wait_all(dve)
            run_chunks(dve, chunk)
            if squares:
                squares.accumulate(dve, KT - 2)
                squares.accumulate(dve, KT - 1)



CONV = 4
QK_PIECES = 2 * MH
VO_CHUNKS = 4
VO_PIECES = 4 * VO_CHUNKS
VW = DV + 1


def mlstm_in_phase(nc, xT, total, norm_gain, ones, ident, qk_pieces, vo_pieces, gate_w, conv_w, conv_b, out_gain, hT_hi, hT_lo, qk, v1, gates, og_dram):
    with ExitStack() as ctx:
        sb = lambda n, s, d=F32: ctx.enter_context(nc.sbuf_tensor(f"mi_{n}", s, d))
        sem = ctx.enter_context(phase_semaphores(nc, "mi_"))
        raw = sb("raw", [P, 2, DM])
        w_hi = sb("w_hi", [P, 2, DM], F32R)
        w_lo = sb("w_lo", [P, 2, DM], F32R)
        g_raw = sb("g_raw", [P, KT, 2 * MH])
        g_hi = sb("g_hi", [P, KT, 2 * MH], F32R)
        g_lo = sb("g_lo", [P, KT, 2 * MH], F32R)
        padded = sb("padded", [P, 2, CONV - 1 + SEQ])
        acc = total
        cw = sb("cw", [P, QK_PIECES, CONV])
        cb = sb("cb", [P, QK_PIECES])
        gain = sb("gain", [P, DM])
        sig = sb("sig", [P, 2, HALF])
        gT = sig[0:2 * MH].rearrange("p a c -> p (a c)")
        ps = [ctx.enter_context(nc.psum_tensor(f"mi_ps{i}", [P, HALF], F32)) for i in range(8)]
        raw_in = [sem(f"raw_in{i}") for i in range(2)]
        small_in, zeroed = sem("small_in"), sem("zeroed")
        w_hi_done, w_lo_done, g_hi_done, g_lo_done = sem("w_hi_done"), sem("w_lo_done"), sem("g_hi_done"), sem("g_lo_done")
        product, copied, conved, silu_done, q_scaled = sem("product"), sem("copied"), sem("conved"), sem("silu_done"), sem("q_scaled")
        gate_mm, gT_done, gates_turned = sem("gate_mm"), sem("gT_done"), sem("gates_turned")
        gates_done, tile_mm = sem("gates_done"), sem("tile_mm")
        v_done, sig_done, gained = sem("v_done"), sem("sig_done"), sem("gained")
        OG_SLOTS = 6
        og_slot = [sig[:, i, :] for i in range(2)] + [padded[:, i // 2, (i % 2) * HALF:(i % 2 + 1) * HALF] for i in range(4)]
        og_out = [sem(f"og_out{i}") for i in range(OG_SLOTS)]
        norm = NormInput(nc, ctx, "mi", sem, tiles_of(xT), total, norm_gain, ones,
                         [sig[:, 0], sig[:, 1], padded[:, 1, CONV - 1:CONV - 1 + HALF]], ps[0:2], hT_hi, hT_lo)
        block = ctx.enter_context(nc.Block())
        NP = QK_PIECES + VO_PIECES
        TILES_V = TT * VO_CHUNKS // 2

        @block.sync
        def _(sp):
            def store(tiles):
                for m in tiles:
                    c, t = divmod(m, TT)
                    sp.wait_ge(gained, m + 1)
                    sp.dma_start(og_dram[t, :, c * HALF:(c + 1) * HALF], og_slot[m % OG_SLOTS])\
                        .then_inc(og_out[m % OG_SLOTS], 16)

            norm.load(sp)
            sp.dma_start(cw[:], conv_w).then_inc(small_in, 16)
            sp.dma_start(cb[:], conv_b).then_inc(small_in, 16)
            sp.dma_start(gain[:], out_gain.to_broadcast([P, DM])).then_inc(small_in, 16)
            sp.dma_start(g_raw[:], gate_w).then_inc(small_in, 16)
            for n in range(NP):
                if n >= 2:
                    sp.wait_ge(w_lo_done, n - 1)
                sp.dma_start(raw[:, n % 2, :], qk_pieces[n] if n < QK_PIECES else vo_pieces[n - QK_PIECES])\
                    .then_inc(raw_in[n % 2], 16)
                if n == NP - 2:
                    store(range(TT))
            store(range(TT, TILES_V))
            for i in range(OG_SLOTS):
                sp.wait_ge(og_out[i], 16 * len(range(i, TILES_V, OG_SLOTS)))

        @block.gpsimd
        def _(pool):
            pool.memset(padded[:, :, 0:CONV - 1], 0.0).then_inc(zeroed, 1)
            pool.memset(v1[:, :, :, DV:VW], 1.0).then_inc(zeroed, 1)
            pool.wait_ge(g_hi_done, 1)
            pool.tensor_tensor(g_lo[:], g_raw[:], g_hi[:].bitcast(F32), ALU.subtract).then_inc(g_lo_done, 1)
            for n in range(NP):
                pool.wait_ge(w_hi_done, n + 1)
                pool.tensor_tensor(w_lo[:, n % 2, :], raw[:, n % 2, :], w_hi[:, n % 2, :].bitcast(F32),
                                   ALU.subtract).then_inc(w_lo_done, 1)
                if n < 2:
                    norm.odd_low(pool, n)

        @block.scalar
        def _(act):
            def hi_part(n):
                act.wait_ge(raw_in[n % 2], 16 * (n // 2 + 1))
                last = n - 2 - QK_PIECES
                if last >= 0 and last % 4 == 3:
                    act.wait_ge(tile_mm, TT * (last // 4 + 1))
                elif last >= 0:
                    act.wait_ge(product, QK_PIECES + 3 * (last // 4) + last % 4 + 1)
                elif n >= 2:
                    act.wait_ge(product, n - 1)
                act.copy(w_hi[:, n % 2, :], raw[:, n % 2, :]).then_inc(w_hi_done, 1)

            norm.roots(act)
            act.wait_ge(small_in, 64)
            act.copy(g_hi[:], g_raw[:]).then_inc(g_hi_done, 1)
            hi_part(0)
            norm.high(act, 0)
            hi_part(1)
            norm.high(act, 1)
            norm.wait_all(act)
            for n in range(QK_PIECES):
                if n >= 1:
                    hi_part(n + 1)
                if n == 7:
                    act.wait_ge(gate_mm, 1)
                    for half in range(2):
                        act.copy(gT[:, half * HALF:(half + 1) * HALF], ps[half][0:2 * MH, :]).then_inc(gT_done, 1)
                act.wait_ge(product, n + 1)
                if n >= 2:
                    act.wait_ge(conved, CONV * (n - 1))
                for half in range(2):
                    c0 = CONV - 1 + half * HALF
                    act.copy(padded[:, n % 2, c0:c0 + HALF], ps[(2 * n + half) % 8][:]).then_inc(copied, 1)
                act.wait_ge(conved, CONV * (n + 1))
                act.activation(qk[:, n, :], acc[:], ACT.Silu, bias=cb[:, n:n + 1]).then_inc(silu_done, 1)
            for n in range(VO_PIECES):
                if n + 1 < VO_PIECES:
                    hi_part(QK_PIECES + n + 1)
                c = n // 4
                if n % 4 == 3 and c >= VO_CHUNKS // 2:
                    for t in range(TT):
                        m = TT * (c - VO_CHUNKS // 2) + t
                        act.wait_ge(tile_mm, TT * c + t + 1)
                        if m >= OG_SLOTS:
                            act.wait_ge(og_out[m % OG_SLOTS], 16 * (m // OG_SLOTS))
                        act.activation(og_slot[m % OG_SLOTS], ps[t][:], ACT.Sigmoid).then_inc(sig_done, 1)

        @block.vector
        def _(dve):
            norm.scale(dve)
            norm.wait_all(dve)
            dve.wait_ge(small_in, 64)
            dve.wait_ge(zeroed, 2)
            for n in range(QK_PIECES):
                src = padded[:, n % 2, :]
                dve.wait_ge(copied, 2 * n + 2)
                if n >= 1:
                    dve.wait_ge(silu_done, n)
                dve.tensor_scalar(acc[:], src[:, 0:SEQ], cw[:, n, 0:1], None, ALU.mult).then_inc(conved, 1)
                for w in range(1, CONV):
                    dve.wait_ge(conved, CONV * n + w)
                    dve.scalar_tensor_tensor(acc[:], src[:, w:w + SEQ], cw[:, n, w:w + 1], acc[:],
                                             ALU.mult, ALU.add).then_inc(conved, 1)
                if 1 <= n <= MH:
                    dve.wait_ge(silu_done, n)
                    dve.tensor_scalar(qk[:, n - 1, :], qk[:, n - 1, :], DK ** -0.5, None, ALU.mult).then_inc(q_scaled, 1)
            dve.wait_ge(gates_turned, 1)
            dve.tensor_copy(gates[:], ps[0][:, 0:TT * 2 * MH].rearrange("p (t g) -> p t g", g=2 * MH)).then_inc(gates_done, 1)
            for m in range(TILES_V):
                c, t = divmod(m, TT)
                dve.wait_ge(tile_mm, m + 1)
                dve.tensor_copy(v1[:, t, 2 * c:2 * c + 2, 0:DV],
                                ps[t][:].rearrange("p (h d) -> p h d", d=DV)).then_inc(v_done, 1)
            for m in range(TILES_V):
                c, t = divmod(m, TT)
                dve.wait_ge(sig_done, m + 1)
                dve.tensor_tensor(og_slot[m % OG_SLOTS], og_slot[m % OG_SLOTS], gain[:, c * HALF:(c + 1) * HALF],
                                  ALU.mult).then_inc(gained, 1)
            dve.wait_ge(v_done, TILES_V)

        @block.tensor
        def _(pe):
            norm.sums(pe)
            for n in range(QK_PIECES):
                pe.wait_ge(w_lo_done, n + 1)
                if n >= 4:
                    pe.wait_ge(copied, 2 * (n - 4) + 2)
                for half in range(2):
                    cols = slice(half * HALF, (half + 1) * HALF)
                    for k in range(KT):
                        rows = slice(k * P, (k + 1) * P)
                        if n == 0:
                            norm.wait_tile(pe, half, k)
                        mm = split_matmul(pe, ps[(2 * n + half) % 8][:], w_hi[:, n % 2, rows], w_lo[:, n % 2, rows],
                                          hT_hi[:, k, cols], hT_lo[:, k, cols], k == 0, k == KT - 1)
                mm.then_inc(product, 1)
                if n == 5:
                    pe.wait_ge(g_lo_done, 1)
                    pe.wait_ge(copied, 2 * 5)
                    for half in range(2):
                        cols = slice(half * HALF, (half + 1) * HALF)
                        for k in range(KT):
                            mm = split_matmul(pe, ps[half][0:2 * MH, :], g_hi[:, k, :], g_lo[:, k, :],
                                              hT_hi[:, k, cols], hT_lo[:, k, cols], k == 0, k == KT - 1)
                    mm.then_inc(gate_mm, 1)
            pe.wait_ge(gT_done, 2)
            for t in range(TT):
                mm = pe.transpose(ps[0][:, t * 2 * MH:(t + 1) * 2 * MH], gT[:, t * P:(t + 1) * P],
                                  ident[0:2 * MH, 0:2 * MH])
            mm.then_inc(gates_turned, 1)
            for n in range(VO_PIECES):
                c = n // 4
                pe.wait_ge(w_lo_done, QK_PIECES + n + 1)
                for kk in range(2):
                    k = 2 * (n % 4) + kk
                    cols = slice(kk * HALF, (kk + 1) * HALF)
                    for t in range(TT):
                        if k == 0:
                            if c == 0:
                                pe.wait_ge(gates_done, 1)
                                pe.wait_ge(copied, 2 * QK_PIECES)
                            elif c <= VO_CHUNKS // 2:
                                pe.wait_ge(v_done, TT * (c - 1) + t + 1)
                            else:
                                pe.wait_ge(sig_done, TT * (c - 1 - VO_CHUNKS // 2) + t + 1)
                        mm = split_matmul(pe, ps[t][:], hT_hi[:, k, t * P:(t + 1) * P], hT_lo[:, k, t * P:(t + 1) * P],
                                          w_hi[:, (QK_PIECES + n) % 2, cols], w_lo[:, (QK_PIECES + n) % 2, cols],
                                          k == 0, k == KT - 1)
                        if k == KT - 1:
                            mm.then_inc(tile_mm, 1)
                if n % 4 != 3:
                    mm.then_inc(product, 1)


def mlstm_cell_phase(nc, ones, ident, gates, gate_bias, qk, v1, og_dram, yT):
    with ExitStack() as ctx:
        sb = lambda n, s, d=F32: ctx.enter_context(nc.sbuf_tensor(f"mc_{n}", s, d))
        psum = lambda n, s: ctx.enter_context(nc.psum_tensor(f"mc_{n}", s, F32))
        sem = ctx.enter_context(phase_semaphores(nc, "mc_"))
        CH = CHUNKS * MH
        gb = sb("gb", [P, 2 * MH])
        upto = sb("upto", [P, P])
        mask = sb("mask", [P, MH, P])
        size = sb("size", [P, CHUNKS, MH])
        low = sb("low", [P, CHUNKS, MH])
        log_f = sb("log_f", [P, CHUNKS, MH])
        b_sum = sb("b_sum", [P, CHUNKS, MH])
        b_last = sb("b_last", [P, CHUNKS, MH])
        a = sb("a", [P, CHUNKS, MH])
        a_row = sb("a_row", [P, CHUNKS, MH, P])
        a_max = sb("a_max", [P, CHUNKS, MH])
        run_max = sb("run_max", [P, CHUNKS, MH])
        m_before = sb("m_before", [P, CHUNKS + 1, MH])
        A = sb("A", [P, CHUNKS, MH])
        neg_A = sb("neg_A", [P, CHUNKS, MH])
        inter = sb("inter", [P, CHUNKS, MH])
        floor = sb("floor", [P, CHUNKS, MH])
        decay = sb("decay", [P, CHUNKS, MH])
        key_w = sb("key_w", [P, CHUNKS, MH])
        state = sb("state", [P, MH, VW])
        E = sb("E", [P, 2, MH, P])
        spread = E
        W = sb("W", [P, MH, P])
        WT = sb("WT", [P, MH, P])
        kw = sb("kw", [P, 2, MH, P])
        carried = sb("carried", [P, 2, VW])
        num = sb("num", [P, 2, MH, VW])
        og = sb("og", [P, 2, DM])
        junk = sb("junk", [P, DV])
        r_den = sb("r_den", [P, MH])
        sums = sb("sums", [P, MH])
        rms = sb("rms", [P, MH])
        factor = sb("factor", [P, MH])
        minus_half = sb("minus_half", [P, MH])
        y = sb("y", [P, DM])
        ps_s = psum("ps_s", [P, HALF])
        ps_k = psum("ps_k", [P, HALF])
        ps_w = psum("ps_w", [P, HALF])
        ps_in = [psum(f"ps_in{i}", [P, HALF]) for i in range(2)]
        ps_st = [psum(f"ps_st{i}", [P, HALF]) for i in range(2)]
        ps_d = psum("ps_d", [P, HALF])
        gb_in = sem("gb_in")
        og_in = [sem(f"og_in{i}") for i in range(2)]
        built, prep, lut, cums = sem("built"), sem("prep"), sem("lut"), sem("cums")
        spread_done, rows_mm, row_read = sem("spread_done"), sem("rows_mm"), sem("row_read")
        chain, ready, exps = sem("chain"), sem("ready"), sem("exps")
        E_done, scored, k_turned, W_done, W_turned = sem("E_done"), sem("scored"), sem("k_turned"), sem("W_done"), sem("W_turned")
        WT_done, kw_done, within, from_state, grown = sem("WT_done"), sem("kw_done"), sem("within"), sem("from_state"), sem("grown")
        carried_done, num_done, state_done = sem("carried_done"), sem("num_done"), sem("state_done")
        tail, summed, root = sem("tail"), sem("summed"), sem("root")
        y_done, y_turned, y_kept = sem("y_done"), sem("y_turned"), sem("y_kept")
        block = ctx.enter_context(nc.Block())
        flat = lambda t: t[:].rearrange("p c h -> p (c h)")

        @block.sync
        def _(sp):
            sp.dma_start(gb[:], gate_bias.to_broadcast([P, 2 * MH])).then_inc(gb_in, 16)
            for c in range(CHUNKS):
                if c >= 2:
                    sp.wait_ge(og_in[c % 2], 16 * (c // 2))
                    sp.wait_ge(y_done, MH * (c - 1))
                sp.dma_start(og[:, c % 2, :], og_dram[c]).then_inc(og_in[c % 2], 16)

        @block.gpsimd
        def _(pool):
            pool.memset(minus_half[:], -0.5).then_inc(built, 1)
            pool.memset(upto[:], 1.0).then_inc(built, 1)
            pool.memset(mask[:], 0.0).then_inc(built, 1)
            pool.memset(m_before[:, 0, :], 0.0).then_inc(built, 1)
            pool.memset(state[:], 0.0).then_inc(built, 1)
            pool.memset(sums[:], 0.0).then_inc(built, 1)
            pool.wait_ge(built, 6)
            pool.affine_select(out=upto[:], in_=upto[:], compare_op=ALU.is_ge, fill=0.0, base=0,
                               pattern=[[1, P]], channel_multiplier=-1).then_inc(built, 1)
            for h in range(MH):
                pool.affine_select(out=mask[:, h, :], in_=mask[:, h, :], compare_op=ALU.is_ge, fill=MASKED, base=0,
                                   pattern=[[-1, P]], channel_multiplier=1).then_inc(built, 1)
            for c in range(CHUNKS):
                pool.wait_ge(prep, 6)
                if c >= 2:
                    pool.wait_ge(rows_mm, c - 1)
                pool.tensor_tensor(spread[:, c % 2], ident[:].rearrange("p (o s) -> p o s", o=1).to_broadcast([P, MH, P]),
                                   a[:, c, :].rearrange("p (h o) -> p h o", o=1).to_broadcast([P, MH, P]), ALU.mult)\
                    .then_inc(spread_done, 1)
            for c in range(CHUNKS):
                pool.wait_ge(tail, 5 * c + 4)
                if c >= 1:
                    pool.wait_ge(tail, 5 * c)
                pool.tensor_tensor(rms[:], sums[:], minus_half[:], ALU.pow).then_inc(root, 1)

        @block.scalar
        def _(act):
            act.wait_ge(prep, 2)
            act.activation(size[:], size[:], ACT.Exp, scale=-1.0).then_inc(lut, 1)
            act.wait_ge(prep, 3)
            act.activation(size[:], size[:], ACT.Ln).then_inc(lut, 1)
            act.wait_ge(built, 11)
            act.wait_ge(ready, 1)
            act.activation(inter[:], inter[:], ACT.Exp).then_inc(exps, 1)
            act.activation(floor[:], floor[:], ACT.Exp, scale=-1.0).then_inc(exps, 1)
            act.activation(decay[:], decay[:], ACT.Exp).then_inc(exps, 1)
            act.activation(key_w[:], key_w[:], ACT.Exp).then_inc(exps, 1)

            def key_weights(c):
                if c >= 2:
                    act.wait_ge(W_done, c - 1)
                else:
                    act.wait_ge(rows_mm, CHUNKS)
                for h in range(MH):
                    act.activation(E[:, c % 2, h, :], a_row[:, c, h, :], ACT.Exp, bias=neg_A[:, c, h:h + 1])\
                       .then_inc(E_done, 1)

            def turned_weights(c):
                act.wait_ge(W_turned, c + 1)
                act.copy(WT[:], ps_w[:].rearrange("p (h s) -> p h s", h=MH)).then_inc(WT_done, 1)

            def carry(c, h):
                n = MH * c + h
                act.wait_ge(from_state, n + 1)
                if n >= 2:
                    act.wait_ge(num_done, n - 1)
                act.activation(carried[:, n % 2, :], ps_st[n % 2][:, 0:VW], ACT.Copy,
                               scale=inter[:, c, h:h + 1]).then_inc(carried_done, 1)

            def square_sums(c):
                act.wait_ge(tail, 5 * c + 3)
                for h in range(MH):
                    if h or c:
                        act.wait_ge(summed, MH * c + h)
                    act.activation(junk[:], num[:, c % 2, h, 0:DV], ACT.Square, scale=r_den[:, h:h + 1],
                                   accum_out=sums[:, h:h + 1]).then_inc(summed, 1)

            def keep_y(c, part):
                act.wait_ge(y_turned, 2 * c + part + 1)
                act.copy(yT[:, 4 * part:4 * part + 4, c * P:(c + 1) * P],
                         ps_w[:].rearrange("p (k t) -> p k t", k=4)).then_inc(y_kept, 1)

            key_weights(0)
            key_weights(1)
            turned_weights(0)
            for c in range(CHUNKS + 2):
                for part in range(2):
                    if c < CHUNKS:
                        carry(c, 2 * part)
                        carry(c, 2 * part + 1)
                    if part == 0 and 1 <= c <= CHUNKS:
                        square_sums(c - 1)
                    if c >= 2:
                        keep_y(c - 2, part)
                if c + 2 < CHUNKS:
                    key_weights(c + 2)
                if c + 1 < CHUNKS:
                    turned_weights(c + 1)

        @block.vector
        def _(dve):
            def rows(c):
                dve.wait_ge(rows_mm, c + 1)
                bank = ps_in[c % 2][:].rearrange("p (h s) -> p h s", h=MH)
                dve.tensor_reduce(a_max[:, c, :], bank, AX.X, ALU.max)
                for h in range(MH):
                    ins = dve.tensor_tensor_reduce(a_row[:, c, h, :], bank[:, h, :], mask[:, h, :], 1.0, -3.0e38,
                                                   ALU.add, ALU.max, run_max[:, c, h:h + 1])
                ins.then_inc(row_read, 1)

            dve.wait_ge(gb_in, 16)
            gi, gf = gates[:, :, 0:MH], gates[:, :, MH:2 * MH]
            dve.tensor_tensor(gates[:], gates[:],
                              gb[:].rearrange("p (o g) -> p o g", o=1).to_broadcast([P, CHUNKS, 2 * MH]), ALU.add)\
                .then_inc(prep, 1)
            dve.wait_ge(prep, 1)
            dve.tensor_scalar(low[:], gf, 0.0, None, ALU.min)
            dve.scalar_tensor_tensor(size[:], gf, -1.0, gf, ALU.mult, ALU.max).then_inc(prep, 1)
            dve.wait_ge(lut, 1)
            dve.tensor_scalar(size[:], size[:], 1.0, None, ALU.add).then_inc(prep, 1)
            dve.wait_ge(lut, 2)
            dve.tensor_tensor(log_f[:], low[:], size[:], ALU.subtract).then_inc(prep, 1)
            dve.wait_ge(cums, 2)
            dve.tensor_copy(flat(b_sum), ps_s[:, 0:CH])
            dve.tensor_copy(flat(b_last), ps_k[:, 0:CH]).then_inc(prep, 1)
            dve.wait_ge(prep, 5)
            dve.tensor_tensor(a[:], gi, b_sum[:], ALU.subtract).then_inc(prep, 1)
            dve.wait_ge(prep, 6)
            dve.wait_ge(built, 11)
            for c in range(CHUNKS):
                rows(c)
            n = 0
            for c in range(CHUNKS):
                if n:
                    dve.wait_ge(chain, n)
                dve.wait_ge(row_read, CHUNKS)
                dve.tensor_tensor(m_before[:, c + 1, :], m_before[:, c, :], a_max[:, c, :], ALU.max).then_inc(chain, 1)
                dve.wait_ge(chain, n + 1)
                dve.tensor_tensor(m_before[:, c + 1, :], m_before[:, c + 1, :], b_last[:, c, :], ALU.add).then_inc(chain, 1)
                n += 2
            dve.wait_ge(chain, n)
            before, after = m_before[:, 0:CHUNKS, :], m_before[:, 1:CHUNKS + 1, :]
            dve.tensor_tensor(A[:], before, run_max[:], ALU.max).then_inc(chain, 1)
            dve.tensor_tensor(decay[:], before, after, ALU.subtract).then_inc(chain, 1)
            dve.tensor_tensor(key_w[:], b_last[:], after, ALU.subtract).then_inc(chain, 1)
            dve.wait_ge(chain, n + 3)
            dve.tensor_scalar(neg_A[:], A[:], -1.0, None, ALU.mult)
            dve.tensor_tensor(inter[:], before, A[:], ALU.subtract)
            dve.tensor_tensor(floor[:], b_sum[:], A[:], ALU.add)
            dve.tensor_tensor(decay[:], decay[:], b_last[:], ALU.add)
            dve.tensor_tensor(key_w[:], key_w[:], a[:], ALU.add).then_inc(ready, 1)
            dve.wait_ge(exps, 4)

            def weigh_scores(c):
                dve.wait_ge(scored, c + 1)
                dve.wait_ge(E_done, MH * (c + 1))
                if c >= 1:
                    dve.wait_ge(W_turned, c)
                dve.tensor_tensor(W[:], ps_s[:].rearrange("p (h s) -> p h s", h=MH), E[:, c % 2], ALU.mult).then_inc(W_done, 1)

            def weigh_keys(c):
                dve.wait_ge(k_turned, c + 1)
                if c >= 2:
                    dve.wait_ge(grown, MH * (c - 1))
                dve.tensor_tensor(kw[:, c % 2], ps_k[:].rearrange("p (h s) -> p h s", h=MH),
                                  key_w[:, c, :].rearrange("p (h o) -> p h o", o=1).to_broadcast([P, MH, P]), ALU.mult)\
                    .then_inc(kw_done, 1)

            def head(c, h):
                n = MH * c + h
                dve.wait_ge(carried_done, n + 1)
                dve.wait_ge(within, n + 1)
                if c >= 2:
                    dve.wait_ge(y_done, n - 2 * MH + 1)
                dve.tensor_tensor(num[:, c % 2, h, :], ps_in[n % 2][:, 0:VW], carried[:, n % 2, :], ALU.add)\
                    .then_inc(num_done, 1)
                dve.wait_ge(grown, n + 1)
                if c >= 1:
                    dve.wait_ge(state_done, n - MH + 1)
                dve.scalar_tensor_tensor(state[:, h, :], state[:, h, :], decay[:, c, h:h + 1], ps_d[:, 0:VW],
                                         ALU.mult, ALU.add).then_inc(state_done, 1)

            def denominators(c):
                dve.wait_ge(num_done, MH * (c + 1))
                if c >= 1:
                    dve.wait_ge(tail, 5 * c)
                den = num[:, c % 2, :, DV]
                dve.scalar_tensor_tensor(r_den[:], den, -1.0, floor[:, c, :], ALU.mult, ALU.max).then_inc(tail, 1)
                dve.wait_ge(tail, 5 * c + 1)
                dve.tensor_tensor(r_den[:], r_den[:], den, ALU.max).then_inc(tail, 1)
                dve.wait_ge(tail, 5 * c + 2)
                dve.reciprocal(r_den[:], r_den[:]).then_inc(tail, 1)

            def mean_squares(c):
                dve.wait_ge(summed, MH * (c + 1))
                dve.tensor_scalar(sums[:], sums[:], 1.0 / DV, EPS, ALU.mult, ALU.add).then_inc(tail, 1)

            def factors(c):
                dve.wait_ge(root, c + 1)
                if c >= 1:
                    dve.wait_ge(y_done, MH * c)
                dve.tensor_tensor(factor[:], r_den[:], rms[:], ALU.mult).then_inc(tail, 1)

            def outputs(c):
                dve.wait_ge(tail, 5 * c + 5)
                dve.wait_ge(og_in[c % 2], 16 * (c // 2 + 1))
                if c >= 1:
                    dve.wait_ge(y_turned, 2 * c)
                for h in range(MH):
                    dve.scalar_tensor_tensor(y[:, h * DV:(h + 1) * DV], num[:, c % 2, h, 0:DV], factor[:, h:h + 1],
                                             og[:, c % 2, h * DV:(h + 1) * DV], ALU.mult, ALU.mult).then_inc(y_done, 1)

            weigh_scores(0)
            weigh_keys(0)
            for c in range(CHUNKS + 1):
                for h in range(MH):
                    if c < CHUNKS:
                        head(c, h)
                    if h == 0 and c + 1 < CHUNKS:
                        weigh_scores(c + 1)
                    if h == 1 and c + 1 < CHUNKS:
                        weigh_keys(c + 1)
                    if h == 2 and c >= 1:
                        mean_squares(c - 1)
                if c >= 1:
                    factors(c - 1)
                if c < CHUNKS:
                    denominators(c)
                if c >= 1:
                    outputs(c - 1)

        @block.tensor
        def _(pe):
            pe.wait_ge(prep, 4)
            pe.wait_ge(built, 7)
            pe.matmul(ps_s[:, 0:CH], upto[:], flat(log_f), start=True, stop=True).then_inc(cums, 1)
            pe.matmul(ps_k[:, 0:CH], ones[:], flat(log_f), start=True, stop=True).then_inc(cums, 1)
            for c in range(CHUNKS):
                pe.wait_ge(spread_done, c + 1)
                if c >= 2:
                    pe.wait_ge(row_read, c - 1)
                pe.matmul(ps_in[c % 2][:], ones[:], spread[:, c % 2].rearrange("p h s -> p (h s)"),
                          start=True, stop=True).then_inc(rows_mm, 1)
            pe.wait_ge(prep, 5)
            pe.wait_ge(row_read, CHUNKS)

            def scores(c):
                cols = slice(c * P, (c + 1) * P)
                if c >= 1:
                    pe.wait_ge(W_done, c)
                for h in range(MH):
                    mm = pe.matmul(ps_s[:, h * P:(h + 1) * P], qk[:, h, cols], qk[:, MH + h, cols], start=True, stop=True)
                mm.then_inc(scored, 1)
                if c >= 1:
                    pe.wait_ge(kw_done, c)
                for h in range(MH):
                    mm = pe.transpose(ps_k[:, h * P:(h + 1) * P], qk[:, MH + h, cols], ident[:])
                mm.then_inc(k_turned, 1)

            def turn_weights(c):
                pe.wait_ge(W_done, c + 1)
                if c >= 1:
                    pe.wait_ge(WT_done, c)
                if c >= 3:
                    pe.wait_ge(y_kept, 2 * c - 4)
                for h in range(MH):
                    mm = pe.transpose(ps_w[:, h * P:(h + 1) * P], W[:, h, :], ident[:])
                mm.then_inc(W_turned, 1)

            def head(c, h):
                n = MH * c + h
                if n >= 2:
                    pe.wait_ge(carried_done, n - 1)
                if c >= 1:
                    pe.wait_ge(state_done, n - MH + 1)
                pe.matmul(ps_st[n % 2][:, 0:VW], qk[:, h, c * P:(c + 1) * P], state[:, h, :], start=True, stop=True)\
                    .then_inc(from_state, 1)
                pe.wait_ge(WT_done, c + 1)
                if n >= 2:
                    pe.wait_ge(num_done, n - 1)
                pe.matmul(ps_in[n % 2][:, 0:VW], WT[:, h, :], v1[:, c, h, :], start=True, stop=True).then_inc(within, 1)
                pe.wait_ge(kw_done, c + 1)
                if n >= 1:
                    pe.wait_ge(state_done, n)
                pe.matmul(ps_d[:, 0:VW], kw[:, c % 2, h, :], v1[:, c, h, :], start=True, stop=True).then_inc(grown, 1)

            def turn_y(c, part):
                pe.wait_ge(y_done, MH * c + 2 * part + 2)
                pe.wait_ge(WT_done, min(c + 3, CHUNKS))
                if c or part:
                    pe.wait_ge(y_kept, 2 * c + part)
                for j in range(4):
                    f = 4 * part + j
                    mm = pe.transpose(ps_w[:, j * P:(j + 1) * P], y[:, f * P:(f + 1) * P], ident[:])
                mm.then_inc(y_turned, 1)

            scores(0)
            turn_weights(0)
            for c in range(CHUNKS + 2):
                if c + 1 < CHUNKS:
                    scores(c + 1)
                for part in range(2):
                    if c < CHUNKS:
                        head(c, 2 * part)
                        head(c, 2 * part + 1)
                    if c >= 2:
                        turn_y(c - 2, part)
                if c + 1 < CHUNKS:
                    turn_weights(c + 1)


def mlstm_phases(nc, xT, total, ones, ident, norm_gain, qk_pieces, vo_pieces, gate_w, conv_w, conv_b, out_gain, gate_bias, keep):
    og_dram = nc.dram_tensor("og_dram", [TT, P, DM], F32, kind="Internal").ap()
    with ExitStack() as ctx:
        qk = ctx.enter_context(nc.sbuf_tensor("mlstm_qk", [P, QK_PIECES, SEQ], F32))
        v1 = ctx.enter_context(nc.sbuf_tensor("mlstm_v1", [P, TT, MH, VW], F32))
        gates = ctx.enter_context(nc.sbuf_tensor("mlstm_gates", [P, TT, 2 * MH], F32))
        with split_hidden(nc, "mlstm") as (hT_hi, hT_lo):
            mlstm_in_phase(nc, xT, total, norm_gain, ones, ident, qk_pieces, vo_pieces, gate_w, conv_w, conv_b, out_gain, hT_hi, hT_lo, qk, v1, gates, og_dram)
        yT = keep.enter_context(nc.sbuf_tensor("mlstm_yT", [P, KT, SEQ], F32, side="right"))
        mlstm_cell_phase(nc, ones, ident, gates, gate_bias, qk, v1, og_dram, yT)
    return yT


@contextmanager
def split_hidden(nc, name):
    with nc.sbuf_tensor(f"{name}_hT_hi", [P, KT, SEQ], F32R) as hi, nc.sbuf_tensor(f"{name}_hT_lo", [P, KT, SEQ], F32R) as lo:
        yield hi, lo


def trunk(nc, xT_in, mixer_gain, mlp_gain, rel_bias, onehot, wqkv, q_gain, k_gain, attn_wo, qk_pieces, vo_pieces,
          gate_w, gate_bias, conv_w, conv_b, out_gain, mlstm_wo, w1, w2, out):
    bias_dram = nc.dram_tensor("bias_dram", [NG, HEADS, BIAS_LEN], F32, kind="Internal").ap()
    yT_dram = nc.dram_tensor("yT_dram", [PAIRS, P, SEQ], F32, kind="Internal").ap()
    with ExitStack() as ctx:
        ones = ctx.enter_context(nc.sbuf_tensor("ones", [P, P], F32))
        ident = ctx.enter_context(nc.sbuf_tensor("ident", [P, P], F32))
        total = ctx.enter_context(nc.sbuf_tensor("total", [P, SEQ], F32, side="right"))
        with ExitStack() as first:
            buffers = AttentionBuffers(nc, first)
            hT_hi, hT_lo = first.enter_context(split_hidden(nc, "attn"))
            constants_phase(nc, ones, ident, rel_bias, onehot, bias_dram, xT_in, buffers.x_tiles, total)
            attention_phase(nc, ones, ident, buffers, total, mixer_gain[0], hT_hi, hT_lo, wqkv, q_gain, k_gain, bias_dram, yT_dram)
        xT = ctx.enter_context(nc.sbuf_tensor("xT", [P, KT, SEQ], F32, side="right"))
        project_phase(nc, "attn_out", xT, total, attn_wo, None, yT_dram, xT_in)
        with split_hidden(nc, "mlp0") as (hT_hi, hT_lo):
            mlp_phase(nc, "mlp0", xT, total, mlp_gain[0], ones, w1[0], w2[0], hT_hi, hT_lo, None)
        with ExitStack() as keep:
            yT = mlstm_phases(nc, xT, total, ones, ident, mixer_gain[1], qk_pieces, vo_pieces, gate_w, conv_w, conv_b,
                              out_gain, gate_bias, keep)
            project_phase(nc, "mlstm_out", xT, total, mlstm_wo, yT, None, None)
        with split_hidden(nc, "mlp1") as (hT_hi, hT_lo):
            mlp_phase(nc, "mlp1", xT, total, mlp_gain[1], ones, w1[1], w2[1], hT_hi, hT_lo, out)



def stationary_pieces(w):
    return np.ascontiguousarray(w.reshape(KT, P, KT, P).transpose(2, 1, 0, 3)).reshape(KT, P, DM)


def kernel(x, mixer_norm, mlp_norm, rel_bias, attn_w_in, attn_q_gain, attn_k_gain, attn_w_out, mlstm_w_in,
           mlstm_gate_bias, mlstm_conv_w, mlstm_conv_b, mlstm_out_gain, mlstm_w_out, mlp_w_in, mlp_w_out):
    import concourse.bacc as bacc
    from concourse.bass_utils import run_bass_kernel_spmd

    depth = mlp_w_in.shape[0]
    lay = np.ascontiguousarray
    w_in = mlstm_w_in[0]
    per_tile = lambda v: lay(v.reshape(-1, KT, P).transpose(0, 2, 1))
    arrays = {
        "xT_in": lay(x[0].T),
        "mixer_gain": per_tile(mixer_norm),
        "mlp_gain": per_tile(mlp_norm),
        "rel_bias": lay(rel_bias),
        "onehot": bias_onehot(),
        "wqkv": lay(attn_w_in[0].reshape(KT, P, 3, NG, PAIRS, P).transpose(4, 3, 0, 1, 2, 5)).reshape(SECTIONS * KT, P, 3 * P),
        "q_gain": lay(attn_q_gain[0].T),
        "k_gain": lay(attn_k_gain[0].T),
        "attn_wo": stationary_pieces(attn_w_out[0]),
        "qk_pieces": stationary_pieces(w_in[:, :DM]),
        "vo_pieces": lay(w_in[:, DM:3 * DM].reshape(4, 2, P, VO_CHUNKS, HALF).transpose(3, 0, 2, 1, 4)).reshape(VO_PIECES, P, DM),
        "gate_w": lay(w_in[:, 3 * DM:].reshape(KT, P, 2 * MH).transpose(1, 0, 2)),
        "gate_bias": lay(mlstm_gate_bias),
        "conv_w": lay(mlstm_conv_w[0].reshape(CONV, KT, P).transpose(2, 1, 0)),
        "conv_b": lay(mlstm_conv_b[0].reshape(KT, P).T),
        "out_gain": lay(mlstm_out_gain[0].reshape(1, DM)),
        "mlstm_wo": stationary_pieces(mlstm_w_out[0]),
        "w1": lay(mlp_w_in.reshape(depth, KT, P, FCH, KT, P).transpose(0, 3, 4, 2, 1, 5)).reshape(depth, FCH, KT, P, DM),
        "w2": lay(mlp_w_out.reshape(depth, FCH, KT, P, KT, P).transpose(0, 1, 4, 3, 2, 5)).reshape(depth, FCH, KT, P, DM),
    }
    nc = bacc.Bacc("TRN2", target_bir_lowering=False, num_devices=1)
    args = {n: nc.dram_tensor(f"in_{n}", a.shape, mybir.dt.from_np(a.dtype), kind="ExternalInput").ap()
            for n, a in arrays.items()}
    out = nc.dram_tensor("out_xT", [KT, P, SEQ], F32, kind="ExternalOutput").ap()
    trunk(nc, **args, out=out)
    r = run_bass_kernel_spmd(nc, [{f"in_{n}": a for n, a in arrays.items()}], core_ids=[0])
    return lay(r.results[0]["out_xT"].reshape(DM, SEQ).T).reshape(1, SEQ, DM)
```
